# Optimizing a Trainium2 kernel written in Bass

```python
import jax, jax.numpy as jnp
from jax import lax
import numpy as np

D_MODEL = 1024
BATCH = 1
SEQ = 1024
DEPTH = 1
DEC_BATCH = 1
DEC_SEQ = 64
PAST_LEN = 2048

CHUNK = 64
MIX_WIDTH = D_MODEL
DN_HEADS = 4
DN_DK = 128
DN_DV = 128
DN_QK = DN_HEADS * DN_DK
DN_WIDTH = DN_HEADS * DN_DV
DN_CONV_CH = 2 * DN_QK + DN_WIDTH
CONV_W = 4
AT_HEADS = 8
AT_DH = 64
AT_WIDTH = AT_HEADS * AT_DH
BAND_CHUNKS = 8
WINDOW = BAND_CHUNKS * CHUNK
BAND = (BAND_CHUNKS + 1) * CHUNK
MAX_REL = 128
N_REL = 2 * MAX_REL + 1
PEER_HEADS = 8
N_KEYS = 128
N_EXPERTS = N_KEYS * N_KEYS
PEER_TOPK = 16
PEER_DKEY = 256
PEER_HALF = PEER_DKEY // 2
PEER_BLOCK = 256
EPS = 1e-6
IN_WIDTH = 3 * AT_WIDTH + DN_CONV_CH + DN_WIDTH + 2 * DN_HEADS
SPLIT_POINTS = [AT_WIDTH, 2 * AT_WIDTH, 3 * AT_WIDTH, 3 * AT_WIDTH + DN_CONV_CH,
                3 * AT_WIDTH + DN_CONV_CH + DN_WIDTH, 3 * AT_WIDTH + DN_CONV_CH + DN_WIDTH + DN_HEADS]

kernel_name = 'hybrid_deltanet_chunkband_peer_step'

def rms_norm(x, g):
    xf = x.astype(jnp.float32)
    y = xf * lax.rsqrt(jnp.mean(xf * xf, axis=-1, keepdims=True) + EPS)
    return (y * g.astype(jnp.float32)).astype(x.dtype)

def l2_norm(x):
    xf = x.astype(jnp.float32)
    return xf * lax.rsqrt(jnp.sum(xf * xf, axis=-1, keepdims=True) + EPS)

def causal_conv(u, prefix, w):
    full = jnp.concatenate([prefix.astype(u.dtype), u], axis=1)
    L = u.shape[1]
    y = full[:, 0:L] * w[0]
    for i in range(1, CONV_W):
        y = y + full[:, i:i + L] * w[i]
    return jax.nn.silu(y), full[:, full.shape[1] - (CONV_W - 1):]

def gated_delta_chunked(q, k, v, g, beta, s0):
    B, L, H, DK = k.shape
    pad = (-L) % CHUNK

    def padt(t):
        return jnp.pad(t, [(0, 0), (0, pad)] + [(0, 0)] * (t.ndim - 2))

    q, k, v, g, beta = padt(q), padt(k), padt(v), padt(g), padt(beta)
    n = (L + pad) // CHUNK

    def chunks(t):
        return jnp.transpose(t.reshape(B, n, CHUNK, H, -1), (1, 0, 3, 2, 4))

    q = chunks(q) * (DK ** -0.5)
    k = chunks(k)
    v = chunks(v)
    g = chunks(g[..., None])[..., 0]
    beta = chunks(beta[..., None])[..., 0]
    gc = jnp.cumsum(g, axis=-1)
    idx = jnp.arange(CHUNK)
    causal = idx[:, None] >= idx[None, :]
    strict = idx[:, None] > idx[None, :]
    decay = jnp.exp(jnp.where(causal, gc[..., :, None] - gc[..., None, :], -jnp.inf))
    kk = jnp.einsum('nbhid,nbhjd->nbhij', k, k)
    A = jnp.where(strict, beta[..., :, None] * kk * decay, 0.0)
    eye = jnp.eye(CHUNK, dtype=jnp.float32)
    T = lax.linalg.triangular_solve(eye + A, jnp.broadcast_to(eye, A.shape), left_side=True,
                                    lower=True, unit_diagonal=True)
    u = T @ (v * beta[..., None])
    w = T @ (k * (beta * jnp.exp(gc))[..., None])
    qk = jnp.where(causal, jnp.einsum('nbhid,nbhjd->nbhij', q, k) * decay, 0.0)

    def step(S, inp):
        q_i, k_i, u_i, w_i, qk_i, gc_i = inp
        v_new = u_i - w_i @ S
        o = (q_i * jnp.exp(gc_i)[..., None]) @ S + qk_i @ v_new
        g_last = gc_i[..., -1]
        k_dec = k_i * jnp.exp(g_last[..., None] - gc_i)[..., None]
        S = S * jnp.exp(g_last)[..., None, None] + jnp.einsum('bhcd,bhce->bhde', k_dec, v_new)
        return S, o

    S, o = lax.scan(step, s0, (q, k, u, w, qk, gc))
    o = jnp.transpose(o, (1, 0, 3, 2, 4)).reshape(B, n * CHUNK, H, -1)[:, :L]
    return o, S

def deltanet_group(qkv_raw, z, b_raw, a_raw, conv_prefix, s0, conv_w, a_log, dt_bias, dn_norm):
    B, L, _ = qkv_raw.shape
    qkv, conv_new = causal_conv(qkv_raw, conv_prefix, conv_w)
    q = l2_norm(qkv[..., :DN_QK].reshape(B, L, DN_HEADS, DN_DK))
    k = l2_norm(qkv[..., DN_QK:2 * DN_QK].reshape(B, L, DN_HEADS, DN_DK))
    v = qkv[..., 2 * DN_QK:].reshape(B, L, DN_HEADS, DN_DV).astype(jnp.float32)
    beta = jax.nn.sigmoid(b_raw.astype(jnp.float32))
    g = -jnp.exp(a_log.astype(jnp.float32)) * jax.nn.softplus(a_raw.astype(jnp.float32) + dt_bias.astype(jnp.float32))
    o, S = gated_delta_chunked(q, k, v, g, beta, s0.astype(jnp.float32))
    zf = z.reshape(B, L, DN_HEADS, DN_DV).astype(jnp.float32)
    o = rms_norm(o, dn_norm) * jax.nn.silu(zf)
    return o.reshape(B, L, DN_WIDTH).astype(qkv_raw.dtype), conv_new, S.astype(s0.dtype)

def rel_bias_table(bias, q_pos, k_pos):
    d = jnp.clip(q_pos[:, None] - k_pos[None, :], -MAX_REL, MAX_REL) + MAX_REL
    return bias[:, d].astype(jnp.float32)

def band_attention_prompt(q, k, v, bias):
    B, S, H, D = q.shape
    n = S // CHUNK
    padc = [(0, 0), (BAND_CHUNKS, 0), (0, 0), (0, 0), (0, 0)]
    kc = jnp.pad(k.reshape(B, n, CHUNK, H, D), padc)
    vc = jnp.pad(v.reshape(B, n, CHUNK, H, D), padc)
    band_idx = jnp.arange(n)[:, None] + jnp.arange(BAND_CHUNKS + 1)[None, :]
    kb = kc[:, band_idx].reshape(B, n, BAND, H, D)
    vb = vc[:, band_idx].reshape(B, n, BAND, H, D)
    s = jnp.einsum('bnqhd,bnkhd->bnhqk', q.reshape(B, n, CHUNK, H, D), kb).astype(jnp.float32) * (D ** -0.5)
    s = s + rel_bias_table(bias, WINDOW + jnp.arange(CHUNK), jnp.arange(BAND))
    valid = jnp.repeat(band_idx >= BAND_CHUNKS, CHUNK, axis=1)
    s = jnp.where(valid[None, :, None, None, :], s, -jnp.inf)
    p = jax.nn.softmax(s, axis=-1).astype(v.dtype)
    return jnp.einsum('bnhqk,bnkhd->bnqhd', p, vb).reshape(B, S, H, D)

def band_attention_step(q, k, v, k_past, v_past, bias):
    P = k_past.shape[1]
    L = q.shape[1]
    D = q.shape[-1]
    kk = jnp.concatenate([k_past.astype(k.dtype), k], axis=1)
    vv = jnp.concatenate([v_past.astype(v.dtype), v], axis=1)
    s = jnp.einsum('bqhd,bkhd->bhqk', q, kk).astype(jnp.float32) * (D ** -0.5)
    s = s + rel_bias_table(bias, P + jnp.arange(L), jnp.arange(P + L))
    p = jax.nn.softmax(s, axis=-1).astype(v.dtype)
    return jnp.einsum('bhqk,bkhd->bqhd', p, vv)

def peer(h, peer_wq, peer_keys, peer_u, peer_v):
    B, L, D = h.shape
    t = h.reshape(B * L, D)
    T = t.shape[0]
    pad = (-T) % PEER_BLOCK
    t = jnp.pad(t, ((0, pad), (0, 0))).reshape(-1, PEER_BLOCK, D)

    def block(xb):
        qh = (xb @ peer_wq).reshape(PEER_BLOCK, PEER_HEADS, 2, PEER_HALF)
        s = jnp.einsum('thpc,hpkc->thpk', qh, peer_keys).astype(jnp.float32)
        sv, si = lax.top_k(s, PEER_TOPK)
        cand = sv[:, :, 0, :, None] + sv[:, :, 1, None, :]
        cid = si[:, :, 0, :, None] * N_KEYS + si[:, :, 1, None, :]
        cv, ci = lax.top_k(cand.reshape(PEER_BLOCK, PEER_HEADS, PEER_TOPK * PEER_TOPK), PEER_TOPK)
        eid = jnp.take_along_axis(cid.reshape(PEER_BLOCK, PEER_HEADS, -1), ci, axis=-1)
        gate = jax.nn.softmax(cv, axis=-1).reshape(PEER_BLOCK, -1)
        eid = eid.reshape(PEER_BLOCK, -1)
        u = jnp.take(peer_u, eid, axis=0)
        vv = jnp.take(peer_v, eid, axis=0)
        a = jax.nn.gelu(jnp.einsum('td,ted->te', xb, u).astype(jnp.float32), approximate=False) * gate
        return jnp.einsum('te,ted->td', a.astype(xb.dtype), vv)

    out = lax.map(block, t).reshape(-1, D)[:T]
    return out.reshape(B, L, D)

def layer(x, conv_prefix, s0, k_past, v_past, ln1, w_in, conv_w, a_log, dt_bias, dn_norm, q_norm, k_norm,
          rel_bias, attn_norm, w_out, ln2, peer_wq, peer_keys, peer_u, peer_v):
    B, L, _ = x.shape
    h = rms_norm(x, ln1)
    proj = h @ w_in
    aq, ak, av, dqkv, dz, db, da = jnp.split(proj, SPLIT_POINTS, axis=-1)
    aq = rms_norm(aq.reshape(B, L, AT_HEADS, AT_DH), q_norm)
    ak = rms_norm(ak.reshape(B, L, AT_HEADS, AT_DH), k_norm)
    av = av.reshape(B, L, AT_HEADS, AT_DH)
    if k_past is None:
        ao = band_attention_prompt(aq, ak, av, rel_bias)
        keep = min(WINDOW, L)
        k_new, v_new = ak[:, L - keep:], av[:, L - keep:]
    else:
        ao = band_attention_step(aq, ak, av, k_past, v_past, rel_bias)
        k_new, v_new = ak, av
    ao = rms_norm(ao.reshape(B, L, AT_WIDTH), attn_norm)
    do, conv_new, s_new = deltanet_group(dqkv, dz, db, da, conv_prefix, s0, conv_w, a_log, dt_bias, dn_norm)
    x = x + jnp.concatenate([ao, do], axis=-1) @ w_out
    x = x + peer(rms_norm(x, ln2), peer_wq, peer_keys, peer_u, peer_v)
    return x, k_new, v_new, conv_new, s_new

def setup_inputs(seed: int = 0) -> dict:
    key = jax.random.key(seed)
    ks = jax.random.split(key, 24)
    f32 = jnp.float32
    nrm = lambda k, shape, s: jax.random.normal(k, shape, f32) * s
    P = min(WINDOW, PAST_LEN)
    dt = jnp.exp(jax.random.uniform(ks[5], (DEPTH, DN_HEADS), f32, np.log(1e-3), np.log(1e-1)))
    return {
        'x_prompt': nrm(ks[0], (BATCH, SEQ, D_MODEL), 1.0),
        'x_sample': nrm(ks[1], (DEC_BATCH, DEC_SEQ, D_MODEL), 1.0),
        'cache_attn_k': nrm(ks[2], (DEPTH, DEC_BATCH, P, AT_HEADS, AT_DH), 1.0),
        'cache_attn_v': nrm(ks[3], (DEPTH, DEC_BATCH, P, AT_HEADS, AT_DH), 1.0),
        'state_dn_conv': nrm(ks[4], (DEPTH, DEC_BATCH, CONV_W - 1, DN_CONV_CH), 1.0),
        'state_dn': nrm(ks[6], (DEPTH, DEC_BATCH, DN_HEADS, DN_DK, DN_DV), 0.3),
        'ln1': 1.0 + nrm(ks[7], (DEPTH, D_MODEL), 0.02),
        'w_in': nrm(ks[8], (DEPTH, D_MODEL, IN_WIDTH), D_MODEL ** -0.5),
        'conv_w': nrm(ks[9], (DEPTH, CONV_W, DN_CONV_CH), CONV_W ** -0.5),
        'a_log': jnp.log(jax.random.uniform(ks[10], (DEPTH, DN_HEADS), f32, 1.0, 16.0)),
        'dt_bias': dt + jnp.log(-jnp.expm1(-dt)),
        'dn_norm': 1.0 + nrm(ks[11], (DEPTH, DN_DV), 0.02),
        'q_norm': 1.0 + nrm(ks[12], (DEPTH, AT_DH), 0.02),
        'k_norm': 1.0 + nrm(ks[13], (DEPTH, AT_DH), 0.02),
        'rel_bias': nrm(ks[14], (DEPTH, AT_HEADS, N_REL), 0.1),
        'attn_norm': 1.0 + nrm(ks[15], (DEPTH, AT_WIDTH), 0.02),
        'w_out': nrm(ks[16], (DEPTH, MIX_WIDTH, D_MODEL), MIX_WIDTH ** -0.5),
        'ln2': 1.0 + nrm(ks[17], (DEPTH, D_MODEL), 0.02),
        'peer_wq': nrm(ks[18], (DEPTH, D_MODEL, PEER_HEADS * PEER_DKEY), D_MODEL ** -0.5),
        'peer_keys': nrm(ks[19], (DEPTH, PEER_HEADS, 2, N_KEYS, PEER_HALF), PEER_HALF ** -0.5),
        'peer_u': nrm(ks[20], (DEPTH, N_EXPERTS, D_MODEL), D_MODEL ** -0.5),
        'peer_v': nrm(ks[21], (DEPTH, N_EXPERTS, D_MODEL), 0.5),
    }

def reference(x_prompt, x_sample, cache_attn_k, cache_attn_v, state_dn_conv, state_dn, ln1, w_in, conv_w,
              a_log, dt_bias, dn_norm, q_norm, k_norm, rel_bias, attn_norm, w_out, ln2, peer_wq, peer_keys,
              peer_u, peer_v):
    yp, ys = x_prompt, x_sample
    Bp = x_prompt.shape[0]
    pk, pv, pc, ps, sk, sv, sc, ss = [], [], [], [], [], [], [], []
    for l in range(DEPTH):
        lw = (ln1[l], w_in[l], conv_w[l], a_log[l], dt_bias[l], dn_norm[l], q_norm[l], k_norm[l], rel_bias[l],
              attn_norm[l], w_out[l], ln2[l], peer_wq[l], peer_keys[l], peer_u[l], peer_v[l])
        zero_conv = jnp.zeros((Bp, CONV_W - 1, DN_CONV_CH), x_prompt.dtype)
        zero_state = jnp.zeros((Bp, DN_HEADS, DN_DK, DN_DV), state_dn.dtype)
        yp, k1, v1, c1, s1 = layer(yp, zero_conv, zero_state, None, None, *lw)
        ys, k2, v2, c2, s2 = layer(ys, state_dn_conv[l], state_dn[l], cache_attn_k[l], cache_attn_v[l], *lw)
        pk.append(k1); pv.append(v1); pc.append(c1); ps.append(s1)
        sk.append(k2); sv.append(v2); sc.append(c2); ss.append(s2)
    return (yp, ys, jnp.stack(pk), jnp.stack(pv), jnp.stack(pc), jnp.stack(ps),
            jnp.stack(sk), jnp.stack(sv), jnp.stack(sc), jnp.stack(ss))


_drawn_inputs = setup_inputs


def setup_inputs(seed=0):
    import zlib

    import numpy as np

    out = dict(_drawn_inputs(seed))
    spreads = {}
    factors = {}
    for name, (base, spread) in spreads.items():
        noise = np.random.default_rng([zlib.crc32(name.encode()), seed]).standard_normal(out[name].shape)
        drawn = base * np.exp(spread * noise) if base else spread * noise
        out[name] = __import__('jax').numpy.asarray(drawn.astype(out[name].dtype))
    for name, factor in factors.items():
        out[name] = (out[name] * factor).astype(out[name].dtype)
    return out
```

```python
from contextlib import ExitStack

import numpy as np

import concourse.bass as bass
from concourse import mybir

F32 = mybir.dt.float32
F32R = mybir.dt.float32r
U32 = mybir.dt.uint32
ALU = mybir.AluOpType
ACT = mybir.ActivationFunctionType
AX = mybir.AxisListType

P = 128
D = 1024
KD = D // P
SEQ = 1024
DEC = 64
TOK = SEQ + DEC
PT = SEQ // P
NT = PT + 1
PADTOK = NT * P
CHUNK = 64
H_AT = 8
DH = 64
H_DN = 4
DK = 128
AT_W = H_AT * DH
DN_W = H_DN * DK
CONV_W = 4
HALO = CONV_W - 1
CONV_CH = 3 * DN_W
CONV_BLOCKS = CONV_CH // P
IN_W = 3 * AT_W + CONV_CH + DN_W + 2 * H_DN
C_AK, C_AV, C_DN, C_Z = AT_W, 2 * AT_W, 3 * AT_W, 3 * AT_W + CONV_CH
C_B = C_Z + DN_W
C_A = C_B + H_DN
WINDOW = 8 * CHUNK
PAST_TILES = WINDOW // P
BAND_TILES = PAST_TILES + 1
BAND = BAND_TILES * P
MAX_REL = 128
N_REL = 2 * MAX_REL + 1
PH = 8
NK = 128
TOPK = 16
EPS = 1e-6
NEG = -1e30
COLS = 512
TAIL = IN_W % COLS
FULL_BLOCKS = IN_W // COLS
LEVELS = 7
RING = 3


def rows_of(t):
    return P if t < PT else DEC


class Steps:

    def __init__(self, sem, names):
        self.sem, self.names, self.emitted = sem, list(names), 0

    def at(self, t, name):
        return t * len(self.names) + self.names.index(name) + 1

    def one(self, name):
        assert self.names[self.emitted % len(self.names)] == name, name
        self.emitted += 1
        return 1


def reach(eng, sem, value):
    if not (isinstance(value, int) and value <= 0):
        eng.wait_ge(sem, value)


def normed_transposed(nc, tag, source, gain, hi, lo, ident_d, eps_d):
    names_act = ["square", "log", "rstd", "scaled"]
    names_dve = ["gained", "high", "low"]
    with ExitStack() as ctx:
        def sb(name, shape, dt=F32):
            return ctx.enter_context(nc.sbuf_tensor(f"{tag}_{name}", shape, dt))

        def sem(name):
            return ctx.enter_context(nc.semaphore(f"{tag}_{name}"))
        x = sb("x", [P, 3, D])
        junk = sb("junk", [P, D])
        xn = sb("xn", [P, 2, D])
        tmp = sb("tmp", [P, KD, P])
        stat = sb("stat", [P, 3, NT])
        ident = sb("ident", [P, P])
        gain_sb = sb("gain", [P, KD])
        eps = sb("eps", [P, 1])
        psum = ctx.enter_context(nc.psum_tensor(f"{tag}_turned", [P, 2, KD, P], F32))
        consts = sem("consts")
        x_loaded = [sem(f"x_loaded{i}") for i in range(3)]
        act_done = Steps(sem("act_done"), names_act)
        turned = sem("turned")
        dve_done = Steps(sem("dve_done"), names_dve)
        block = ctx.enter_context(nc.Block())

        @block.sync
        def _(sp):
            sp.dma_start(ident[:, :], ident_d).then_inc(consts, 16)
            sp.dma_start(gain_sb[:, :], gain).then_inc(consts, 16)
            with nc.allow_non_contiguous_dma("one number to a partition"):
                sp.dma_start(eps[:, :], eps_d).then_inc(consts, 16)
            for t in range(NT):
                if t >= 3:
                    sp.wait_ge(act_done.sem, act_done.at(t - 3, "scaled"))
                sp.dma_start(x[0:rows_of(t), t % 3, :], source(t)).then_inc(x_loaded[t % 3], 16)

        @block.scalar
        def _(act):
            act.wait_ge(consts, 48)
            for t in range(NT):
                n = rows_of(t)
                act.wait_ge(x_loaded[t % 3], 16 * (t // 3 + 1))
                if t >= 1:
                    act.wait_ge(act_done.sem, act_done.at(t - 1, "square"))
                nc.scalar.activation(junk[0:n, :], x[0:n, t % 3, :], ACT.Square,
                                     accum_out=stat[0:n, 0, t:t + 1]).then_inc(act_done.sem, 1)
                act.wait_ge(act_done.sem, act_done.at(t, "square"))
                nc.scalar.activation(stat[0:n, 1, t:t + 1], stat[0:n, 0, t:t + 1], ACT.Ln,
                                     bias=eps[0:n, :], scale=1.0 / D).then_inc(act_done.sem, 1)
                act.wait_ge(act_done.sem, act_done.at(t, "log"))
                nc.scalar.activation(stat[0:n, 2, t:t + 1], stat[0:n, 1, t:t + 1], ACT.Exp,
                                     scale=-0.5).then_inc(act_done.sem, 1)
                act.wait_ge(act_done.sem, act_done.at(t, "rstd"))
                if t >= 2:
                    act.wait_ge(turned, t - 1)
                nc.scalar.activation(xn[0:n, t % 2, :], x[0:n, t % 3, :], ACT.Copy,
                                     scale=stat[0:n, 2, t:t + 1]).then_inc(act_done.sem, 1)

        @block.tensor
        def _(pe):
            pe.wait_ge(consts, 48)
            for t in range(NT):
                n = rows_of(t)
                pe.wait_ge(act_done.sem, act_done.at(t, "scaled"))
                if t >= 2:
                    pe.wait_ge(dve_done.sem, dve_done.at(t - 2, "gained"))
                for k in range(KD):
                    last = nc.tensor.transpose(psum[:, t % 2, k, 0:n], xn[0:n, t % 2, k * P:(k + 1) * P],
                                               ident[0:n, 0:n])
                last.then_inc(turned, 1)

        @block.vector
        def _(dve):
            if hi.shape[2] > TOK:
                nc.vector.memset(hi[:, :, TOK:].bitcast(F32), 0.0)
                nc.vector.memset(lo[:, :, TOK:].bitcast(F32), 0.0)
            dve.wait_ge(consts, 48)
            for t in range(NT):
                n = rows_of(t)
                cols = slice(t * P, t * P + n)
                dve.wait_ge(turned, t + 1)
                if t >= 1:
                    dve.wait_ge(dve_done.sem, dve_done.at(t - 1, "low"))
                nc.vector.tensor_tensor(tmp[:, :, 0:n], psum[:, t % 2, :, 0:n],
                                        gain_sb[:, :].unsqueeze(2).to_broadcast([P, KD, n]),
                                        ALU.mult).then_inc(dve_done.sem, 1)
                dve.wait_ge(dve_done.sem, dve_done.at(t, "gained"))
                nc.vector.tensor_copy(hi[:, :, cols], tmp[:, :, 0:n]).then_inc(dve_done.sem, 1)
                dve.wait_ge(dve_done.sem, dve_done.at(t, "high"))
                nc.vector.tensor_tensor(lo[:, :, cols], tmp[:, :, 0:n], hi[:, :, cols].bitcast(F32),
                                        ALU.subtract).then_inc(dve_done.sem, 1)


def project(nc, x_tile, ln1, w_in, proj, ident_d, eps_d):
    with ExitStack() as ctx:
        h_hi = ctx.enter_context(nc.sbuf_tensor("h_hi", [P, KD, PADTOK], F32R))
        h_lo = ctx.enter_context(nc.sbuf_tensor("h_lo", [P, KD, PADTOK], F32R))
        normed_transposed(nc, "n1", x_tile, ln1, h_hi, h_lo, ident_d, eps_d)

        def sb(name, shape, dt=F32):
            return ctx.enter_context(nc.sbuf_tensor(f"pj_{name}", shape, dt))

        def sem(name):
            return ctx.enter_context(nc.semaphore(f"pj_{name}"))
        w_raw = sb("w_raw", [P, KD, COLS])
        w_hi = sb("w_hi", [P, 2, KD, COLS], F32R)
        w_lo = sb("w_lo", [P, 2, KD, COLS], F32R)
        out = sb("out", [P, RING, COLS])
        psum = ctx.enter_context(nc.psum_tensor("pj_acc", [P, 4, COLS], F32))
        w_loaded, w_high, w_low = sem("w_loaded"), sem("w_high"), sem("w_low")
        products, copied = sem("products"), sem("copied")
        stored = [sem(f"stored{i}") for i in range(RING)]
        w_view = w_in.rearrange("(k p) n -> p k n", p=P)
        blocks = FULL_BLOCKS + 1

        def width(cb):
            return TAIL if isinstance(cb, int) and cb == FULL_BLOCKS else COLS

        def each_block(eng, body):
            body(0, 0)
            body(1, 1)
            with eng.Fori(1, FULL_BLOCKS // 2) as i:
                body(i * 2, 0)
                body(i * 2 + 1, 1)
            for cb in range(FULL_BLOCKS // 2 * 2, blocks):
                body(cb, cb % 2)

        block = ctx.enter_context(nc.Block())

        @block.sync
        def _(sp):
            def load(cb):
                w = width(cb)
                start = cb * COLS
                sp.dma_start(w_raw[:, :, 0:w], w_view[:, :, bass.ds(start, w)]).then_inc(w_loaded, 16)

            load(0)

            def body(cb, par):
                if not (isinstance(cb, int) and cb == blocks - 1):
                    sp.wait_ge(w_high, cb + 1)
                    sp.wait_ge(w_low, cb + 1)
                    load(cb + 1)
                w = width(cb)
                for t in range(NT):
                    sp.wait_ge(copied, cb * NT + t + 1)
                    with nc.allow_non_contiguous_dma("the last block is 8 columns wide"):
                        sp.dma_start(proj[t * P:(t + 1) * P, bass.ds(cb * COLS, w)],
                                     out[:, t % RING, 0:w]).then_inc(stored[t % RING], 16)
            each_block(sp, body)
            for s in stored:
                sp.wait_ge(s, 16 * (NT // RING) * blocks)

        @block.scalar
        def _(act):
            act.wait_ge(w_loaded, 16)
            nc.scalar.activation(w_hi[:, 0, :, :], w_raw[:, :, :], ACT.Copy).then_inc(w_high, 1)

            def body(cb, par):
                if not (isinstance(cb, int) and cb == blocks - 1):
                    reach(act, products, cb * NT)
                    nxt = cb + 1
                    w = width(nxt)
                    act.wait_ge(w_loaded, cb * 16 + 32)
                    nc.scalar.activation(w_hi[:, 1 - par, :, 0:w], w_raw[:, :, 0:w], ACT.Copy).then_inc(w_high, 1)
                w = width(cb)
                for t in range(NT):
                    act.wait_ge(products, cb * NT + t + 1)
                    reach(act, stored[t % RING], (cb * (NT // RING) + t // RING) * 16)
                    nc.scalar.activation(out[:, t % RING, 0:w], psum[:, t % 4, 0:w], ACT.Copy).then_inc(copied, 1)
            each_block(act, body)

        @block.vector
        def _(dve):
            dve.wait_ge(w_high, 1)
            nc.vector.tensor_tensor(w_lo[:, 0, :, :], w_raw[:, :, :], w_hi[:, 0, :, :].bitcast(F32),
                                    ALU.subtract).then_inc(w_low, 1)

            def body(cb, par):
                if not (isinstance(cb, int) and cb == blocks - 1):
                    w = width(cb + 1)
                    dve.wait_ge(w_high, cb + 2)
                    nc.vector.tensor_tensor(w_lo[:, 1 - par, :, 0:w], w_raw[:, :, 0:w],
                                            w_hi[:, 1 - par, :, 0:w].bitcast(F32), ALU.subtract).then_inc(w_low, 1)
            each_block(dve, body)

        @block.tensor
        def _(pe):
            def body(cb, par):
                w = width(cb)
                pe.wait_ge(w_low, cb + 1)
                for t in range(NT):
                    if t >= 4:
                        pe.wait_ge(copied, cb * NT + t - 3)
                    else:
                        reach(pe, copied, cb * NT)
                    cols = slice(t * P, (t + 1) * P)
                    n = 0
                    for a, b in ((h_hi, w_hi), (h_lo, w_hi), (h_hi, w_lo)):
                        for k in range(KD):
                            last = nc.tensor.matmul(psum[:, t % 4, 0:w], a[:, k, cols], b[:, par, k, 0:w],
                                                    start=(n == 0), stop=(n == 3 * KD - 1))
                            n += 1
                    last.then_inc(products, 1)
            each_block(pe, body)


CHUNKS = ((0, 384), (384, 384), (768, TOK - 768))
CW = 384


def route(nc, h_hi, h_lo, wq, keys, ident_d, iota_d, sel_i, sel_j, sel_g):
    with ExitStack() as ctx:
        def sb(name, shape, dt=F32):
            return ctx.enter_context(nc.sbuf_tensor(f"rt_{name}", shape, dt))

        def sem(name):
            return ctx.enter_context(nc.semaphore(f"rt_{name}"))
        w_raw = sb("w_raw", [P, 2, KD, P])
        w_hi = sb("w_hi", [P, 2, KD, P], F32R)
        w_lo = sb("w_lo", [P, 2, KD, P], F32R)
        keys_sb = sb("keys", [P, 2 * PH, NK])
        ident = sb("ident", [P, P])
        iota = sb("iota", [P, TOPK])
        query = sb("query", [P, PADTOK])
        score = sb("score", [P, 2, NT, NK])
        rest = sb("rest", [P, NT, NK])
        top_v = sb("top_v", [P, 2, NT, TOPK])
        top_i = sb("top_i", [P, 2, NT, TOPK], U32)
        top_f = sb("top_f", [P, 2, NT, TOPK])
        cand = sb("cand", [P, NT, TOPK, TOPK])
        cand2 = sb("cand2", [P, NT, TOPK, TOPK])
        cand_v = sb("cand_v", [P, NT, TOPK])
        cand_i = sb("cand_i", [P, NT, TOPK], U32)
        place = sb("place", [P, 2, NT, TOPK], U32)
        place_f = sb("place_f", [P, 2, NT, TOPK])
        less = sb("less", [P, NT, TOPK])
        expd = sb("expd", [P, NT, TOPK])
        total = sb("total", [P, 2, NT])
        chosen = sb("chosen", [P, 3, NT, PH * TOPK])
        qp = ctx.enter_context(nc.psum_tensor("rt_qp", [P, 3, 512], F32))
        sp_ = ctx.enter_context(nc.psum_tensor("rt_sp", [P, 3, 4, NK], F32))
        consts, cleared, w_loaded = sem("consts"), sem("cleared"), [sem("w_loaded0"), sem("w_loaded1")]
        w_high, w_low, queried, query_out = sem("w_high"), sem("w_low"), sem("queried"), sem("query_out")
        scored, score_out = sem("scored"), sem("score_out")
        top = Steps(sem("top"), ["first8", "rest", "first8_i", "next8", "next8_i"])
        pick_names = ["float", "sums", "first8", "rest", "first8_i", "next8", "next8_i", "place_a", "place_b",
                      "place_f", "less", "eq0", "mul0", "red0", "eq1", "mul1", "red1", "total", "inv", "gate"]
        pick = Steps(sem("pick"), pick_names)
        exps = sem("exps")
        sel_turned, sel_out = sem("sel_turned"), sem("sel_out")
        block = ctx.enter_context(nc.Block())

        @block.sync
        def _(sp):
            sp.dma_start(keys_sb[:, :, :], keys).then_inc(consts, 16)
            sp.dma_start(ident[:, :], ident_d).then_inc(consts, 16)
            sp.dma_start(iota[:, :], iota_d).then_inc(consts, 16)
            for p in range(2):
                sp.dma_start(w_raw[:, p, :, :], wq[p]).then_inc(w_loaded[p], 16)
            with sp.Fori(1, PH) as h:
                for p in range(2):
                    sp.wait_ge(w_high, h * 2 + p - 1)
                    sp.wait_ge(w_low, h * 2 + p - 1)
                    sp.dma_start(w_raw[:, p, :, :], wq[h * 2 + p]).then_inc(w_loaded[p], 16)

        @block.scalar
        def _(act):
            act.wait_ge(cleared, 1)

            def body(h, first):
                for p in range(2):
                    hp = h * 2 + p
                    act.wait_ge(w_loaded[p], h * 16 + 16)
                    if not first:
                        act.wait_ge(queried, hp - 1)
                    nc.scalar.activation(w_hi[:, p, :, :], w_raw[:, p, :, :], ACT.Copy).then_inc(w_high, 1)
                    act.wait_ge(queried, hp + 1)
                    reach(act, scored, hp)
                    for c, (at, n) in enumerate(CHUNKS):
                        last = nc.scalar.activation(query[:, at:at + n], qp[:, c, 0:n], ACT.Copy)
                    last.then_inc(query_out, 1)
                    act.wait_ge(scored, hp + 1)
                    if not first:
                        act.wait_ge(top.sem, top.at(hp - 2, "first8_i"))
                    for c in range(3):
                        n = min(4, NT - 4 * c)
                        last = nc.scalar.activation(score[:, p, 4 * c:4 * c + n, :], sp_[:, c, 0:n, :], ACT.Copy)
                    last.then_inc(score_out, 1)
                act.wait_ge(pick.sem, pick.at(h, "less"))
                nc.scalar.activation(expd[:, :, :], less[:, :, :], ACT.Exp).then_inc(exps, 1)
            body(0, True)
            with act.Fori(1, PH) as h:
                body(h, False)
            for s, dst in enumerate((sel_i, sel_j, sel_g)):
                act.wait_ge(sel_turned, s + 1)
                for c in range(3):
                    n = min(4, NT - 4 * c)
                    last = nc.scalar.activation(dst[:, 4 * c * P:(4 * c + n) * P],
                                                (qp if s % 2 == 0 else sp_.ap().rearrange("p c a b -> p c (a b)"))
                                                [:, c, 0:n * P], ACT.Copy)
                last.then_inc(sel_out, 1)

        @block.tensor
        def _(pe):
            pe.wait_ge(consts, 48)

            def body(h, first):
                for p in range(2):
                    hp = h * 2 + p
                    pe.wait_ge(w_low, hp + 1)
                    if not (first and p == 0):
                        pe.wait_ge(query_out, hp)
                    for c, (at, n) in enumerate(CHUNKS):
                        m = 0
                        for a, b in ((w_hi, h_hi), (w_hi, h_lo), (w_lo, h_hi)):
                            for k in range(KD):
                                last = nc.tensor.matmul(qp[:, c, 0:n], a[:, p, k, :], b[:, k, at:at + n],
                                                        start=(m == 0), stop=(m == 3 * KD - 1))
                                m += 1
                    last.then_inc(queried, 1)
                    pe.wait_ge(query_out, hp + 1)
                    if not (first and p == 0):
                        pe.wait_ge(score_out, hp)
                    for t in range(NT):
                        last = nc.tensor.matmul(sp_[:, t // 4, t % 4, :], query[:, t * P:(t + 1) * P],
                                                keys_sb[:, hp, :] if isinstance(hp, int) else
                                                keys_sb[:, bass.ds(hp, 1), :], start=True, stop=True)
                    last.then_inc(scored, 1)
            body(0, True)
            with pe.Fori(1, PH) as h:
                body(h, False)
            pe.wait_ge(pick.sem, pick.at(PH - 1, "gate"))
            pe.wait_ge(score_out, 2 * PH)
            for s in range(3):
                if s == 2:
                    pe.wait_ge(sel_out, 1)
                for t in range(NT):
                    bank = (qp[:, t // 4, (t % 4) * P:(t % 4 + 1) * P] if s % 2 == 0 else sp_[:, t // 4, t % 4, :])
                    last = nc.tensor.transpose(bank, chosen[:, s, t, :], ident[:, :])
                last.then_inc(sel_turned, 1)

        @block.vector
        def _(dve):
            nc.vector.memset(query[:, TOK:PADTOK], 0.0).then_inc(cleared, 1)
            dve.wait_ge(consts, 48)

            def bc4(ap, dim):
                return ap.unsqueeze(dim).to_broadcast([P, NT, TOPK, TOPK])

            def body(h, first):
                for p in range(2):
                    hp = h * 2 + p
                    dve.wait_ge(w_high, hp + 1)
                    nc.vector.tensor_tensor(w_lo[:, p, :, :], w_raw[:, p, :, :], w_hi[:, p, :, :].bitcast(F32),
                                            ALU.subtract).then_inc(w_low, 1)
                    dve.wait_ge(score_out, hp + 1)
                    if not first:
                        dve.wait_ge(pick.sem, pick.at(h - 1, "mul1"))
                    for t in range(NT):
                        last = nc.vector.max(top_v[:, p, t, 0:8], score[:, p, t, :])
                    last.then_inc(top.sem, 1)
                    dve.wait_ge(top.sem, top.at(hp, "first8"))
                    for t in range(NT):
                        last = nc.vector.match_replace(rest[:, t, :], top_v[:, p, t, 0:8], score[:, p, t, :], NEG)
                    last.then_inc(top.sem, 1)
                    for t in range(NT):
                        last = nc.vector.max_index(top_i[:, p, t, 0:8], top_v[:, p, t, 0:8], score[:, p, t, :])
                    last.then_inc(top.sem, 1)
                    dve.wait_ge(top.sem, top.at(hp, "rest"))
                    for t in range(NT):
                        last = nc.vector.max(top_v[:, p, t, 8:16], rest[:, t, :])
                    last.then_inc(top.sem, 1)
                    dve.wait_ge(top.sem, top.at(hp, "next8"))
                    for t in range(NT):
                        last = nc.vector.max_index(top_i[:, p, t, 8:16], top_v[:, p, t, 8:16], rest[:, t, :])
                    last.then_inc(top.sem, 1)
                    dve.wait_ge(top.sem, top.at(hp, "next8_i"))

                def step(name, ins, wait=True):
                    ins.then_inc(pick.sem, 1)
                    if wait:
                        dve.wait_ge(pick.sem, pick.at(h, name))

                def flat(x, t):
                    return x[:, t, :, :].rearrange("p a b -> p (a b)")
                step("float", nc.vector.tensor_copy(top_f[:, :, :, :], top_i[:, :, :, :]))
                step("sums", nc.vector.tensor_tensor(cand[:, :, :, :], bc4(top_v[:, 0, :, :], 3),
                                                     bc4(top_v[:, 1, :, :], 2), ALU.add))
                for t in range(NT):
                    last = nc.vector.max(cand_v[:, t, 0:8], flat(cand, t))
                step("first8", last)
                for t in range(NT):
                    last = nc.vector.match_replace(flat(cand2, t), cand_v[:, t, 0:8], flat(cand, t), NEG)
                step("rest", last)
                for t in range(NT):
                    last = nc.vector.max_index(cand_i[:, t, 0:8], cand_v[:, t, 0:8], flat(cand, t))
                step("first8_i", last)
                for t in range(NT):
                    last = nc.vector.max(cand_v[:, t, 8:16], flat(cand2, t))
                step("next8", last)
                for t in range(NT):
                    last = nc.vector.max_index(cand_i[:, t, 8:16], cand_v[:, t, 8:16], flat(cand2, t))
                step("next8_i", last)
                step("place_a", nc.vector.tensor_scalar(place[:, 0, :, :], cand_i[:, :, :], 4, None,
                                                        ALU.logical_shift_right), False)
                step("place_b", nc.vector.tensor_scalar(place[:, 1, :, :], cand_i[:, :, :], 15, None,
                                                        ALU.bitwise_and))
                step("place_f", nc.vector.tensor_copy(place_f[:, :, :, :], place[:, :, :, :]), False)
                step("less", nc.vector.tensor_tensor(less[:, :, :], cand_v[:, :, :],
                                                     cand_v[:, :, 0:1].to_broadcast([P, NT, TOPK]), ALU.subtract))
                for q in range(2):
                    step(f"eq{q}", nc.vector.tensor_tensor(
                        cand[:, :, :, :], bc4(place_f[:, q, :, :], 3),
                        iota[:, :].unsqueeze(1).unsqueeze(1).to_broadcast([P, NT, TOPK, TOPK]), ALU.is_equal))
                    step(f"mul{q}", nc.vector.tensor_tensor(cand2[:, :, :, :], cand[:, :, :, :],
                                                            bc4(top_f[:, q, :, :], 2), ALU.mult))
                    step(f"red{q}", nc.vector.tensor_reduce(
                        chosen[:, q, :, bass.ds(h * TOPK, TOPK)], cand2[:, :, :, :], AX.X, ALU.add))
                dve.wait_ge(exps, h + 1)
                step("total", nc.vector.tensor_reduce(total[:, 0, :], expd[:, :, :], AX.X, ALU.add))
                step("inv", nc.vector.reciprocal(total[:, 1, :], total[:, 0, :]))
                step("gate", nc.vector.tensor_tensor(chosen[:, 2, :, bass.ds(h * TOPK, TOPK)], expd[:, :, :],
                                                     total[:, 1, :].unsqueeze(2).to_broadcast([P, NT, TOPK]),
                                                     ALU.mult))
            for h in range(PH):
                body(h, h == 0)
            dve.wait_ge(sel_out, 3)


GB = 64
NB = TOK // GB
JG = 2
GROUPS = NK // JG
OH = 8


def gate_matrices(nc, sel_i, sel_j, sel_g, iota128_d, gates):
    with ExitStack() as ctx:
        def sb(name, shape, dt=F32):
            return ctx.enter_context(nc.sbuf_tensor(f"gt_{name}", shape, dt))

        def sem(name):
            return ctx.enter_context(nc.semaphore(f"gt_{name}"))
        iota = sb("iota", [P, NK])
        one_i = sb("one_i", [P, OH, NK])
        one_j = sb("one_j", [P, OH, NK])
        out = sb("out", [P, NK, GB])
        psum = ctx.enter_context(nc.psum_tensor("gt_psum", [P, 4, 4, NK], F32))
        consts, hot, multiplied, copied, stored = (sem("consts"), sem("hot"), sem("multiplied"), sem("copied"),
                                                   sem("stored"))
        Q = GB // 4
        block = ctx.enter_context(nc.Block())

        @block.sync
        def _(sp):
            sp.dma_start(iota[:, :], iota128_d).then_inc(consts, 16)
            view = gates.rearrange("g i b x -> i g b x")
            with sp.Fori(0, NB) as b:
                sp.wait_ge(copied, b * Q + Q)
                sp.dma_start(view[:, :, bass.ds(b, 1), :].rearrange("i g b x -> i g (b x)"),
                             out[:, :, :].rearrange("p (g j) t -> p g (j t)", j=JG)).then_inc(stored, 16)
            sp.wait_ge(stored, 16 * NB)

        @block.vector
        def _(dve):
            dve.wait_ge(consts, 16)

            def body(b, first):
                for q in range(Q):
                    if not (first and q < 2):
                        dve.wait_ge(multiplied, b * Q + q - 1)
                    for r in range(4):
                        s = (4 * q + r) % OH
                        tok = bass.ds(b * GB + 4 * q + r, 1)
                        nc.vector.tensor_scalar(one_i[:, s, :], iota[:, :], sel_i[:, tok], None, ALU.is_equal)
                        last = nc.vector.tensor_scalar(one_j[:, s, :], iota[:, :], sel_j[:, tok], sel_g[:, tok],
                                                       ALU.is_equal, ALU.mult)
                    last.then_inc(hot, 1)
            body(0, True)
            with dve.Fori(1, NB) as b:
                body(b, False)

        @block.tensor
        def _(pe):
            def body(b, first):
                for q in range(Q):
                    pe.wait_ge(hot, b * Q + q + 1)
                    if not (first and q < 4):
                        pe.wait_ge(copied, b * Q + q - 3)
                    for r in range(4):
                        s = (4 * q + r) % OH
                        last = nc.tensor.matmul(psum[:, q % 4, r, :], one_i[:, s, :], one_j[:, s, :],
                                                start=True, stop=True)
                    last.then_inc(multiplied, 1)
            body(0, True)
            with pe.Fori(1, NB) as b:
                body(b, False)

        @block.scalar
        def _(act):
            def body(b):
                reach(act, stored, b * 16)
                for q in range(Q):
                    act.wait_ge(multiplied, b * Q + q + 1)
                    nc.scalar.activation(out[:, :, 4 * q:4 * q + 4], psum[:, q % 4, :, :].rearrange("p t j -> p j t"),
                                         ACT.Copy).then_inc(copied, 1)
            body(0)
            with act.Fori(1, NB) as b:
                body(b)


def experts(nc, h_hi, h_lo, gates, u, v, x2, ident_d, y_rows):
    NU = JG * len(CHUNKS)
    NV = len(CHUNKS) * KD
    VB = 5
    with ExitStack() as ctx:
        def sb(name, shape, dt=F32):
            return ctx.enter_context(nc.sbuf_tensor(f"ex_{name}", shape, dt))

        def sem(name):
            return ctx.enter_context(nc.semaphore(f"ex_{name}"))
        y = sb("y", [P, KD, TOK])
        u_raw = sb("u_raw", [P, JG, KD, P])
        v_raw = sb("v_raw", [P, JG, D])
        u_hi, u_lo = sb("u_hi", [P, JG, KD, P], F32R), sb("u_lo", [P, JG, KD, P], F32R)
        v_hi, v_lo = sb("v_hi", [P, JG, D], F32R), sb("v_lo", [P, JG, D], F32R)
        gate = sb("gate", [P, NB, JG, GB])
        act_f = sb("act_f", [P, 2, CW])
        gated_f = sb("gated_f", [P, 2, CW])
        a_hi, a_lo = sb("a_hi", [P, JG, TOK], F32R), sb("a_lo", [P, JG, TOK], F32R)
        psum_u = ctx.enter_context(nc.psum_tensor("ex_psum_u", [P, 3, 512], F32))
        psum_v = ctx.enter_context(nc.psum_tensor("ex_psum_v", [P, VB, 512], F32))
        u_loaded, v_loaded, gate_loaded = sem("u_loaded"), sem("v_loaded"), sem("gate_loaded")
        u_high, u_low, v_high, v_low = sem("u_high"), sem("u_low"), sem("v_high"), sem("v_low")
        cleared, hidden, active, gated, a_high, a_low = (sem("cleared"), sem("hidden"), sem("active"), sem("gated"),
                                                         sem("a_high"), sem("a_low"))
        summed, added = sem("summed"), sem("added")
        units = [(j, c) for j in range(JG) for c in range(len(CHUNKS))]

        with nc.Block() as block:
            @block.sync
            def _(sp):
                sp.dma_start(u_raw[:, :, :, :], u[0]).then_inc(u_loaded, 16)

                def body(g, last):
                    reach(sp, gated, g * NU)
                    sp.dma_start(gate[:, :, :, :].rearrange("p b j t -> p b (j t)"), gates[g]).then_inc(gate_loaded, 16)
                    reach(sp, v_high, g)
                    reach(sp, v_low, g)
                    sp.dma_start(v_raw[:, :, :], v[g]).then_inc(v_loaded, 16)
                    if not last:
                        sp.wait_ge(u_high, g + 1)
                        sp.wait_ge(u_low, g + 1)
                        sp.dma_start(u_raw[:, :, :, :], u[g + 1]).then_inc(u_loaded, 16)
                body(0, False)
                with sp.Fori(1, GROUPS - 1) as g:
                    body(g, False)
                body(GROUPS - 1, True)

            @block.scalar
            def _(act):
                act.wait_ge(u_loaded, 16)
                nc.scalar.activation(u_hi[:, :, :, :], u_raw[:, :, :, :], ACT.Copy).then_inc(u_high, 1)

                def high(g, n):
                    j, c = units[n]
                    at, w = CHUNKS[c]
                    act.wait_ge(gated, g * NU + n + 1)
                    nc.scalar.activation(a_hi[:, j, at:at + w], gated_f[:, n % 2, 0:w], ACT.Copy).then_inc(a_high, 1)

                def body(g, last):
                    act.wait_ge(v_loaded, g * 16 + 16)
                    reach(act, summed, g * NV)
                    nc.scalar.activation(v_hi[:, :, :], v_raw[:, :, :], ACT.Copy).then_inc(v_high, 1)
                    for n, (j, c) in enumerate(units):
                        w = CHUNKS[c][1]
                        act.wait_ge(hidden, g * NU + n + 1)
                        if n >= 2:
                            act.wait_ge(gated, g * NU + n - 1)
                        nc.scalar.activation(act_f[:, n % 2, 0:w], psum_u[:, c, 0:w], ACT.Gelu).then_inc(active, 1)
                        if n >= 1:
                            high(g, n - 1)
                    high(g, NU - 1)
                    if not last:
                        act.wait_ge(u_loaded, g * 16 + 32)
                        nc.scalar.activation(u_hi[:, :, :, :], u_raw[:, :, :, :], ACT.Copy).then_inc(u_high, 1)
                body(0, False)
                with act.Fori(1, GROUPS - 1) as g:
                    body(g, False)
                body(GROUPS - 1, True)

            @block.gpsimd
            def _(pool):
                def body(g):
                    pool.wait_ge(gate_loaded, g * 16 + 16)
                    for n, (j, c) in enumerate(units):
                        at, w = CHUNKS[c]
                        pool.wait_ge(active, g * NU + n + 1)
                        if n >= 2:
                            pool.wait_ge(a_low, g * NU + n - 1)
                        else:
                            reach(pool, a_low, g * NU)
                        nc.gpsimd.tensor_tensor(
                            gated_f[:, n % 2, 0:w].rearrange("p (b t) -> p b t", t=GB),
                            act_f[:, n % 2, 0:w].rearrange("p (b t) -> p b t", t=GB),
                            gate[:, at // GB:(at + w) // GB, j, :], ALU.mult).then_inc(gated, 1)
                body(0)
                with pool.Fori(1, GROUPS) as g:
                    body(g)

            @block.vector
            def _(dve):
                nc.vector.memset(y[:, :, :], 0.0).then_inc(cleared, 1)
                dve.wait_ge(cleared, 1)
                dve.wait_ge(u_high, 1)
                nc.vector.tensor_tensor(u_lo[:, :, :, :], u_raw[:, :, :, :], u_hi[:, :, :, :].bitcast(F32),
                                        ALU.subtract).then_inc(u_low, 1)

                def body(g, last):
                    dve.wait_ge(v_high, g + 1)
                    nc.vector.tensor_tensor(v_lo[:, :, :], v_raw[:, :, :], v_hi[:, :, :].bitcast(F32),
                                            ALU.subtract).then_inc(v_low, 1)
                    for n, (j, c) in enumerate(units):
                        at, w = CHUNKS[c]
                        dve.wait_ge(a_high, g * NU + n + 1)
                        nc.vector.tensor_tensor(a_lo[:, j, at:at + w], gated_f[:, n % 2, 0:w],
                                                a_hi[:, j, at:at + w].bitcast(F32), ALU.subtract).then_inc(a_low, 1)
                    if not last:
                        dve.wait_ge(u_high, g + 2)
                        nc.vector.tensor_tensor(u_lo[:, :, :, :], u_raw[:, :, :, :], u_hi[:, :, :, :].bitcast(F32),
                                                ALU.subtract).then_inc(u_low, 1)
                    reach(dve, added, g * NV)
                    n = 0
                    for at, w in CHUNKS:
                        for d in range(KD):
                            dve.wait_ge(summed, g * NV + n + 1)
                            nc.vector.tensor_tensor(y[:, d, at:at + w], y[:, d, at:at + w],
                                                    psum_v[:, n % VB, 0:w], ALU.add).then_inc(added, 1)
                            n += 1
                body(0, False)
                with dve.Fori(1, GROUPS - 1) as g:
                    body(g, False)
                body(GROUPS - 1, True)

            @block.tensor
            def _(pe):
                def body(g):
                    pe.wait_ge(u_low, g + 1)
                    for n, (j, c) in enumerate(units):
                        at, w = CHUNKS[c]
                        if n >= 3:
                            pe.wait_ge(active, g * NU + n - 2)
                        else:
                            reach(pe, active, g * NU)
                        m = 0
                        for k in range(KD):
                            for a, b in ((u_hi, h_hi), (u_hi, h_lo), (u_lo, h_hi)):
                                last = nc.tensor.matmul(psum_u[:, c, 0:w], a[:, j, k, :], b[:, k, at:at + w],
                                                        start=(m == 0), stop=(m == 3 * KD - 1))
                                m += 1
                        last.then_inc(hidden, 1)
                    pe.wait_ge(v_low, g + 1)
                    n = 0
                    for c, (at, w) in enumerate(CHUNKS):
                        pe.wait_ge(a_low, g * NU + len(CHUNKS) * (JG - 1) + c + 1)
                        for d in range(KD):
                            if n >= VB:
                                pe.wait_ge(added, g * NV + n - VB + 1)
                            elif n == 0:
                                reach(pe, added, g * NV)
                            m = 0
                            for j in range(JG):
                                for a, b in ((v_hi, a_hi), (v_hi, a_lo), (v_lo, a_hi)):
                                    last = nc.tensor.matmul(psum_v[:, n % VB, 0:w], a[:, j, d * P:(d + 1) * P],
                                                            b[:, j, at:at + w], start=(m == 0), stop=(m == 3 * JG - 1))
                                    m += 1
                            last.then_inc(summed, 1)
                            n += 1
                body(0)
                with pe.Fori(1, GROUPS) as g:
                    body(g)

        with nc.sbuf_tensor("ex_ident", [P, P], F32) as ident, nc.sbuf_tensor("ex_x", [P, 2, D], F32) as x, \
                nc.Block() as block:
            loaded, stored = [sem("loaded0"), sem("loaded1")], [sem("stored0"), sem("stored1")]
            id_loaded, turned, done = sem("id_loaded"), sem("turned"), sem("done")

            @block.sync
            def _(sp):
                sp.dma_start(ident[:, :], ident_d).then_inc(id_loaded, 16)

                def store(t):
                    sp.wait_ge(done, t + 1)
                    sp.dma_start(y_rows(t), x[0:rows_of(t), t % 2, :]).then_inc(stored[t % 2], 16)
                for t in range(NT):
                    if t >= 2:
                        store(t - 2)
                        sp.wait_ge(stored[t % 2], 16 * (t // 2))
                    sp.dma_start(x[0:rows_of(t), t % 2, :], x2(t)).then_inc(loaded[t % 2], 16)
                store(NT - 2)
                store(NT - 1)
                for i in range(2):
                    sp.wait_ge(stored[i], 16 * ((NT + 1 - i) // 2))

            @block.tensor
            def _(pe):
                pe.wait_ge(id_loaded, 16)
                for t in range(NT):
                    n = rows_of(t)
                    if t >= 2:
                        pe.wait_ge(done, t - 1)
                    for d in range(KD):
                        last = nc.tensor.transpose(psum_v[0:n, 2 * (t % 2) + d // 4, (d % 4) * P:(d % 4 + 1) * P],
                                                   y[:, d, t * P:t * P + n], ident[:, :])
                    last.then_inc(turned, 1)

            @block.vector
            def _(dve):
                for t in range(NT):
                    n = rows_of(t)
                    dve.wait_ge(loaded[t % 2], 16 * (t // 2 + 1))
                    dve.wait_ge(turned, t + 1)
                    xt = x[0:n, t % 2, :].rearrange("p (a b) -> p a b", a=2)
                    nc.vector.tensor_tensor(xt, xt, psum_v[0:n, 2 * (t % 2):2 * (t % 2) + 2, :], ALU.add)\
                        .then_inc(done, 1)


C_IDENT, C_ONES, C_TRI, C_STRICT, C_IOTA, C_FLIP, C_LEVEL = (P * n for n in range(7))
C_OUTSIDE = C_LEVEL + (LEVELS + 1) * P
C_EPS = C_OUTSIDE + BAND
C_LNQ = C_EPS + 1
C_ONE = C_LNQ + 1
C_END = C_ONE + 1
TOE = BAND + P - 1


def constants():
    i, j = np.arange(P)[:, None], np.arange(P)[None, :]
    out = np.zeros((P, C_END), np.float32)
    out[:, C_IDENT:C_IDENT + P] = i == j
    out[:, C_ONES:C_ONES + P] = 1
    out[:, C_TRI:C_TRI + P] = i <= j
    out[:, C_STRICT:C_STRICT + P] = i < j
    out[:, C_IOTA:C_IOTA + P] = j
    out[:, C_FLIP:C_FLIP + P] = i + j == P - 1
    for s in range(LEVELS):
        b = 1 << s
        out[:, C_LEVEL + s * P:C_LEVEL + (s + 1) * P] = (i // (2 * b) == j // (2 * b)) & (i // b % 2 == 1) & (j // b % 2 == 0)
    out[:, C_LEVEL + LEVELS * P:C_LEVEL + (LEVELS + 1) * P] = (i // 2 == j // 2) & (j % 2 == 1) & (i % 2 == 0)
    k = np.arange(BAND)[None, :]
    outside = ((i < CHUNK) & (k >= BAND - CHUNK)) | ((i >= CHUNK) & (k < CHUNK))
    out[:, C_OUTSIDE:C_OUTSIDE + BAND] = np.where(outside, np.float32(NEG), np.float32(0))
    out[:, C_EPS] = EPS
    out[:, C_LNQ] = np.log(DK ** -0.5)
    out[:, C_ONE] = 1
    return out


def relative_bias(nc, bias_flipped, toeplitz, consts_sb, bias):
    with ExitStack() as ctx:
        def sem(name):
            return ctx.enter_context(nc.semaphore(f"rb_{name}"))
        row = ctx.enter_context(nc.sbuf_tensor("rb_row", [H_AT, TOE], F32))
        skew = ctx.enter_context(nc.sbuf_tensor("rb_skew", [P, H_AT, BAND], F32))
        psum = ctx.enter_context(nc.psum_tensor("rb_psum", [P, 4, 512], F32))
        loaded, filled, written, skewed, flipped, masked = (sem("loaded"), sem("filled"), sem("written"),
                                                            sem("skewed"), sem("flipped"), sem("masked"))
        far = TOE - (N_REL - 1)
        parts = [(h, half) for h in range(H_AT) for half in range(2)]
        block = ctx.enter_context(nc.Block())

        @block.sync
        def _(sp):
            sp.dma_start(row[:, far:TOE], bias_flipped[:, 0:N_REL - 1]).then_inc(loaded, 16)
            sp.wait_ge(filled, 1)
            sp.dma_start(toeplitz[:, :], row[:, :]).then_inc(written, 16)
            sp.wait_ge(written, 16)
            src = bass.AP(tensor=toeplitz.tensor, offset=0, ap=[[1, P], [TOE, H_AT], [1, BAND]])
            sp.dma_start(skew[:, :, :], src).then_inc(skewed, 16)

        @block.vector
        def _(dve):
            dve.wait_ge(loaded, 16)
            nc.vector.tensor_copy(row[:, 0:far], row[:, far:far + 1].to_broadcast([H_AT, far])).then_inc(filled, 1)
            for n, (h, half) in enumerate(parts):
                dve.wait_ge(flipped, n + 1)
                cols = slice(half * BAND // 2, (half + 1) * BAND // 2)
                nc.vector.tensor_tensor(bias[:, h, cols], psum[:, n % 4, 0:BAND // 2],
                                        consts_sb[:, C_OUTSIDE:C_OUTSIDE + BAND][:, cols], ALU.add).then_inc(masked, 1)

        @block.tensor
        def _(pe):
            pe.wait_ge(skewed, 16)
            for n, (h, half) in enumerate(parts):
                if n >= 4:
                    pe.wait_ge(masked, n - 3)
                nc.tensor.matmul(psum[:, n % 4, 0:BAND // 2], consts_sb[:, C_FLIP:C_FLIP + P],
                                 skew[:, h, half * BAND // 2:(half + 1) * BAND // 2], start=True, stop=True)\
                    .then_inc(flipped, 1)


def mix(nc, I, proj, toeplitz, x_tile, x2_tile, outs):
    with ExitStack() as ctx:
        def sb(name, shape, dt=F32):
            return ctx.enter_context(nc.sbuf_tensor(f"mx_{name}", shape, dt))

        def sem(name):
            return ctx.enter_context(nc.semaphore(f"mx_{name}"))
        cs = sb("consts", [P, C_END])
        bias = sb("bias", [P, H_AT, BAND])
        head_gain = sb("head_gain", [P, 2 * AT_W])
        conv_w = sb("conv_w", [P, CONV_BLOCKS, CONV_W])
        cat_gain = sb("cat_gain", [P, KD])
        dn_small = sb("dn_small", [P, 4, H_DN])
        w_out = sb("w_out", [P, KD, D])
        consts = sem("consts")
        setup = sem("setup")
        with nc.Block() as block:
            @block.sync
            def _(sp):
                sp.dma_start(cs[:, :], I["consts"]).then_inc(consts, 16)
                for half, name in enumerate(("q_norm", "k_norm")):
                    sp.dma_start(head_gain[:, half * AT_W:(half + 1) * AT_W].rearrange("p (h d) -> p h d", d=DH),
                                 I[name].unsqueeze(0).to_broadcast([P, H_AT, DH])).then_inc(consts, 16)
                sp.dma_start(conv_w[:, :, :], I["conv_w"]).then_inc(consts, 16)
                sp.dma_start(cat_gain[:, 0:H_DN], I["attn_norm"]).then_inc(consts, 16)
                for h in range(H_DN):
                    with nc.allow_non_contiguous_dma("128 numbers, one to a partition"):
                        sp.dma_start(cat_gain[:, H_DN + h:H_DN + h + 1], I["dn_norm"]).then_inc(consts, 16)
                sp.dma_start(dn_small[:, 0, :], I["a_log"].to_broadcast([P, H_DN])).then_inc(consts, 16)
                sp.dma_start(dn_small[:, 1, :], I["dt_bias"].to_broadcast([P, H_DN])).then_inc(consts, 16)
                sp.dma_start(w_out[:, :, :], I["w_out"].rearrange("(k p) n -> p k n", p=P)).then_inc(consts, 16)
                sp.wait_ge(consts, 16 * 12)

            @block.scalar
            def _(act):
                act.wait_ge(consts, 16 * 12)
                nc.scalar.activation(dn_small[:, 2, :], dn_small[:, 0, :], ACT.Exp).then_inc(setup, 1)

            @block.vector
            def _(dve):
                dve.wait_ge(setup, 1)
                nc.vector.tensor_scalar(dn_small[:, 3, :], dn_small[:, 2, :], -1.0, None, ALU.mult).then_inc(setup, 1)
                nc.vector.tensor_scalar(head_gain[:, 0:AT_W], head_gain[:, 0:AT_W], DH ** -0.5, None,
                                        ALU.mult).then_inc(setup, 1)
        relative_bias(nc, I["rel_bias"], toeplitz, cs, bias)
        mix_tiles(nc, I, proj, x_tile, x2_tile, outs, cs, bias, head_gain, conv_w, cat_gain, dn_small, w_out)


def mix_tiles(nc, I, proj, x_tile, x2_tile, outs, cs, bias, head_gain, conv_w, cat_gain, dn_small, w_out):
    ident = cs[:, C_IDENT:C_IDENT + P]
    ones = cs[:, C_ONES:C_ONES + P]
    tri = cs[:, C_TRI:C_TRI + P]
    eps = cs[:, C_EPS:C_EPS + 1]
    lnq = cs[:, C_LNQ:C_LNQ + 1]
    one = cs[:, C_ONE:C_ONE + 1]
    with ExitStack() as ctx:
        def sb(name, shape, dt=F32):
            return ctx.enter_context(nc.sbuf_tensor(f"mx_{name}", shape, dt))

        def sem(name):
            return ctx.enter_context(nc.semaphore(f"mx_{name}"))
        pj = sb("pj", [P, 2, IN_W])
        xt = sb("xt", [P, D])
        wide = sb("wide", [P, 2 * AT_W])
        ssq = sb("ssq", [P, 16])
        ssl = sb("ssl", [P, 16])
        rsq = sb("rsq", [P, 16])
        qkn = sb("qkn", [P, 2 * AT_W])
        past_k = pj[:, 1 - PT % 2, 0:PAST_TILES * AT_W].rearrange("p (m n) -> p m n", m=PAST_TILES)
        qT = sb("qT", [P, 4, P])
        kT = sb("kT", [P, 4, BAND_TILES, P])
        vh = sb("vh", [P, BAND_TILES, AT_W])
        biased = sb("biased", [P, 2, BAND])
        top = sb("top", [P, H_AT])
        ntop = sb("ntop", [P, H_AT])
        prob = sb("prob", [P, 2, BAND])
        sums = sb("sums", [P, H_AT])
        inv = sb("inv", [P, H_AT])
        probT = sb("probT", [P, BAND])
        ao = sb("ao", [P, AT_W])
        stat = sb("stat", [P, 4])
        cat = sb("cat", [P, D])
        cbuf = sb("cbuf", [P, CONV_BLOCKS, HALO + P])
        cy = sb("cy", [P, CONV_BLOCKS, P])
        cc = sb("cc", [P, CONV_BLOCKS, P])
        csq = sb("csq", [P, 8, P])
        cln = cy[:, 0:8, :]
        catT = csq
        qkd = sb("qkd", [P, 8, P])
        small = sb("small", [P, 16, H_DN])
        grow = sb("grow", [P, 4, P])
        egrow = sb("egrow", [P, 4, P])
        brow = sb("brow", [P, 4, P])
        dec = sb("dec", [P, 4, P])
        decT = sb("decT", [P, 4, P])
        m1 = sb("m1", [P, 4, P])
        AT = sb("AT", [P, 4, P])
        QK = sb("QK", [P, 4, P])
        T = sb("T", [P, 4, P])
        Z = sb("Z", [P, 4, P])
        W = sb("W", [P, 4, P])
        kbn = sb("kbn", [P, 4, P])
        vb = sb("vb", [P, 4, P])
        kd = sb("kd", [P, 4, P])
        qg = sb("qg", [P, 4, P])
        wT, vn = m1, grow
        S = sb("S", [P, 4, P])
        oS, osq = brow, dec
        zs = sb("zs", [P, 4, P])
        banks = [ctx.enter_context(nc.psum_tensor(f"mx_bank{n}", [P, w * 512], F32))
                 for n, w in enumerate((2, 2, 1, 1, 1, 1))]
        SC, PTp, OB, X, Y, Zb = banks
        X3, Y3, Z3 = (b.ap().rearrange("p (h n) -> p h n", h=4) for b in (X, Y, Zb))

        lv = [s for s in range(1, LEVELS)]
        pe_names = (["convT", "gcol", "rows", "qkT", "norms", "kvT", "kk", "A"]
                    + [f"{a}{s}" for s in lv for a in ("w", "t", "z")]
                    + ["wT", "vn", "o", "ds"] + [f"{a}{h}" for h in range(H_AT) for a in ("sc", "pt", "pv")]
                    + ["catT", "out"])
        act_names = (["expb", "absexp", "lnsp", "cTc", "silu", "siluz", "sq", "sqln", "rsq", "qkTc", "growc",
                      "browc", "egrow", "expcol", "dec", "csq", "cln", "crs", "wTc", "vnc", "oS", "osq", "oln", "ors"]
                     + [f"{a}{h}" for h in range(H_AT) for a in ("exp", "ptc")] + ["aosq", "aoln", "aors", "cat0"])
        dve_names = (["halo", "eb1", "beta", "apre", "aabs", "amax", "sp", "g", "gz", "conv0", "conv1", "conv2",
                      "conv3", "ssq", "qkn0", "qkn", "gcol", "dif", "glg", "qkd", "decT", "m1", "bneg", "kscale", "kbn",
                      "kd", "vb", "qg", "at0", "AT", "QK", "T0", "T", "Z0", "Z"]
                     + [f"{a}{s}" for s in lv for a in ("W", "T", "Z")] + ["S", "ossq", "oz", "cat1"]
                     + [f"{a}{h}" for h in range(H_AT) for a in ("sm", "nt")] + ["inv", "ao", "catT", "x2"])
        pe_s, act_s, dve_s = (Steps(sem("pe"), pe_names), Steps(sem("act"), act_names), Steps(sem("dve"), dve_names))
        pj_loaded, vh_loaded = [sem("pj_loaded0"), sem("pj_loaded1")], sem("vh_loaded")
        x_loaded, past_loaded, x2_stored, kept = sem("x_loaded"), sem("past_loaded"), sem("x2_stored"), sem("kept")
        k_kept = sem("k_kept")
        state_loaded, past_turned, past_copied, init = (sem("state_loaded"), sem("past_turned"), sem("past_copied"),
                                                        sem("init"))
        block = ctx.enter_context(nc.Block())

        def band(t):
            seen = min(t, PAST_TILES) if t < PT else PAST_TILES
            slots = [(t - seen + n) % BAND_TILES for n in range(seen + 1)]
            return slots, (BAND_TILES - len(slots)) * P

        (EB, EB1, BETA, APRE, AABS, AMAX, AEXP, ASP, SPL, G, GCOL, GLG, EGC, EKD, BNEG, OSS) = range(16)

        @block.sync
        def _(sp):
            def load(t):
                sp.dma_start(pj[:, t % 2, :], proj[t * P:(t + 1) * P, :]).then_inc(pj_loaded[t % 2], 16)
            load(0)
            sp.wait_ge(init, 1)
            n_kept = 0
            for t in range(NT):
                n = rows_of(t)
                if t >= 1:
                    sp.wait_ge(dve_s.sem, dve_s.at(t - 1, "x2"))
                sp.dma_start(vh[:, t % BAND_TILES, :], proj[t * P:(t + 1) * P, C_AV:C_AV + AT_W]).then_inc(vh_loaded, 16)
                if t == PT:
                    for m in range(PAST_TILES):
                        slot = (t - PAST_TILES + m) % BAND_TILES
                        sp.dma_start(vh[:, slot, :], I["cache_v"][m * P:(m + 1) * P, :]).then_inc(past_loaded, 16)
                        sp.dma_start(past_k[:, m, :], I["cache_k"][m * P:(m + 1) * P, :]).then_inc(past_loaded, 16)
                    sp.dma_start(outs["p_state"].rearrange("h k v -> k h v"), S[:, :, :]).then_inc(kept, 16)
                    n_kept += 1
                    sp.wait_ge(kept, 16 * n_kept)
                    sp.dma_start(S[:, :, :], I["state"].rearrange("h k v -> k h v")).then_inc(state_loaded, 16)
                    with nc.allow_non_contiguous_dma("three rows before the sample's"):
                        sp.dma_start(cbuf[:, :, 0:HALO], I["conv_state"]).then_inc(state_loaded, 16)
                sp.dma_start(xt[0:n, :], x_tile(t)).then_inc(x_loaded, 16)
                if t + 1 < NT:
                    load(t + 1)
                if t >= PT - PAST_TILES:
                    sp.wait_ge(dve_s.sem, dve_s.at(t, "qkn"))
                    dst = outs["p_k"][(t - PT + PAST_TILES) * P:(t - PT + PAST_TILES + 1) * P, :] if t < PT else outs["s_k"]
                    sp.dma_start(dst, qkn[0:n, AT_W:2 * AT_W]).then_inc(k_kept, 16)
                    dst = outs["p_v"][(t - PT + PAST_TILES) * P:(t - PT + PAST_TILES + 1) * P, :] if t < PT else outs["s_v"]
                    sp.dma_start(dst, pj[0:n, t % 2, C_AV:C_AV + AT_W]).then_inc(kept, 16)
                    n_kept += 1
                if t >= PT - 1:
                    dst = outs["p_conv"] if t < PT else outs["s_conv"]
                    sp.dma_start(dst, pj[n - HALO:n, t % 2, C_DN:C_DN + CONV_CH]).then_inc(kept, 16)
                    n_kept += 1
                    sp.wait_ge(kept, 16 * n_kept)
                elif t >= PT - PAST_TILES:
                    sp.wait_ge(kept, 16 * n_kept)
                sp.wait_ge(dve_s.sem, dve_s.at(t, "x2"))
                sp.dma_start(x2_tile(t), xt[0:n, :]).then_inc(x2_stored, 16)
                sp.wait_ge(x2_stored, 16 * (t + 1))
            sp.dma_start(outs["s_state"].rearrange("h k v -> k h v"), S[:, :, :]).then_inc(kept, 16)
            sp.wait_ge(kept, 16 * (n_kept + 1))
            sp.wait_ge(k_kept, 16 * (NT - PT + PAST_TILES))

        @block.scalar
        def _(act):
            for t in range(NT):
                par = t % 2
                pt = pj[:, par, :]

                def on(steps, name, tt=t):
                    act.wait_ge(steps.sem, steps.at(tt, name))

                def step(name, out, in_, func, **kw):
                    nc.scalar.activation(out, in_, func, **kw).then_inc(act_s.sem, act_s.one(name))
                if t >= 1:
                    on(dve_s, "x2", t - 1)
                act.wait_ge(pj_loaded[par], 16 * (t // 2 + 1))
                step("expb", small[:, EB, :], pt[:, C_B:C_B + H_DN], ACT.Exp, scale=-1.0)
                on(dve_s, "aabs")
                step("absexp", small[:, AEXP, :], small[:, AABS, :], ACT.Exp, scale=-1.0)
                on(act_s, "absexp")
                step("lnsp", small[:, SPL, :], small[:, AEXP, :], ACT.Ln, bias=one)
                on(pe_s, "convT")
                on(dve_s, "halo")
                for n, b in enumerate((X3, Y3, Z3)):
                    last = nc.scalar.activation(cbuf[:, 4 * n:4 * n + 4, HALO:], b, ACT.Copy)
                last.then_inc(act_s.sem, act_s.one("cTc"))
                on(dve_s, "conv3")
                step("silu", cc[:, :, :], cy[:, :, :], ACT.Silu)
                step("siluz", zs[:, :, :].rearrange("p h n -> p (h n)"), pt[:, C_Z:C_Z + DN_W], ACT.Silu)
                step("sq", wide[:, :], pt[:, 0:2 * AT_W], ACT.Square)
                on(dve_s, "ssq")
                step("sqln", ssl[:, :], ssq[:, :], ACT.Ln, scale=1.0 / DH, bias=eps)
                on(act_s, "sqln")
                step("rsq", rsq[:, :], ssl[:, :], ACT.Exp, scale=-0.5)
                on(pe_s, "qkT")
                nc.scalar.activation(qT[:, :, :], SC[:, 0:512].rearrange("p (a n) -> p a n", a=4), ACT.Copy)
                step("qkTc", kT[:, :, t % BAND_TILES, :], SC[:, 512:1024].rearrange("p (a n) -> p a n", a=4), ACT.Copy)
                if t == PT:
                    for m in range(PAST_TILES):
                        act.wait_ge(past_turned, m + 1)
                        nc.scalar.activation(kT[:, :, (t - PAST_TILES + m) % BAND_TILES, :],
                                             SC[:, 512 * (m % 2):512 * (m % 2) + 512].rearrange("p (a n) -> p a n", a=4),
                                             ACT.Copy).then_inc(past_copied, 1)
                on(pe_s, "rows")
                step("growc", grow[:, :, :], Y3, ACT.Copy)
                step("browc", brow[:, :, :], Z3, ACT.Copy)
                on(act_s, "growc")
                step("egrow", egrow[:, :, :], grow[:, :, :], ACT.Exp)
                on(dve_s, "glg")
                step("expcol", small[:, EGC:EKD + 1, :], small[:, GCOL:GLG + 1, :], ACT.Exp)
                step("dec", dec[:, :, :], dec[:, :, :], ACT.Exp)
                on(act_s, "silu")
                step("csq", csq[:, :, :], cc[:, 0:8, :], ACT.Square)
                on(pe_s, "norms")
                nc.scalar.activation(cln[:, 0:4, :], X3, ACT.Ln, bias=eps)
                step("cln", cln[:, 4:8, :], Y3, ACT.Ln, bias=eps)
                on(act_s, "cln")
                nc.scalar.activation(csq[:, 0:4, :], cln[:, 0:4, :], ACT.Exp, scale=-0.5, bias=lnq)
                step("crs", csq[:, 4:8, :], cln[:, 4:8, :], ACT.Exp, scale=-0.5)
                on(pe_s, "wT")
                step("wTc", wT[:, :, :], X3, ACT.Copy)
                on(pe_s, "vn")
                step("vnc", vn[:, :, :], Y3, ACT.Copy)
                on(pe_s, "o")
                step("oS", oS[:, :, :], Z3, ACT.Copy)
                on(act_s, "oS")
                step("osq", osq[:, :, :], oS[:, :, :], ACT.Square)
                on(dve_s, "ossq")
                step("oln", small[:, EB, :], small[:, OSS, :], ACT.Ln, scale=1.0 / DK, bias=eps)
                on(act_s, "oln")
                step("ors", small[:, EB1, :], small[:, EB, :], ACT.Exp, scale=-0.5)
                slots, at = band(t)
                nk = len(slots) * P
                for h in range(H_AT):
                    on(dve_s, f"nt{h}")
                    if h >= 2:
                        on(pe_s, f"pt{h - 2}")
                    step(f"exp{h}", prob[:, h % 2, 0:nk], biased[:, h % 2, 0:nk], ACT.Exp, bias=ntop[:, h:h + 1],
                         accum_out=sums[:, h:h + 1])
                    on(pe_s, f"pt{h}")
                    if h >= 1:
                        on(pe_s, f"pv{h - 1}")
                    step(f"ptc{h}", probT[:, 0:nk], PTp[:, 0:nk], ACT.Copy)
                on(dve_s, "ao")
                step("aosq", wide[:, 0:AT_W], ao[:, :], ACT.Square, accum_out=stat[:, 0:1])
                on(act_s, "aosq")
                step("aoln", stat[:, 1:2], stat[:, 0:1], ACT.Ln, scale=1.0 / AT_W, bias=eps)
                on(act_s, "aoln")
                step("aors", stat[:, 2:3], stat[:, 1:2], ACT.Exp, scale=-0.5)
                on(act_s, "aors")
                step("cat0", cat[:, 0:AT_W], ao[:, :], ACT.Copy, scale=stat[:, 2:3])

        @block.vector
        def _(dve):
            nc.vector.memset(S[:, :, :], 0.0)
            nc.vector.memset(xt[:, :], 0.0)
            nc.vector.memset(cbuf[:, :, 0:HALO], 0.0).then_inc(init, 1)
            dve.wait_ge(init, 1)

            def level(s):
                return cs[:, C_LEVEL + s * P:C_LEVEL + (s + 1) * P].unsqueeze(1).to_broadcast([P, 4, P])
            ident4 = ident.unsqueeze(1).to_broadcast([P, 4, P])
            for t in range(NT):
                par = t % 2
                pt = pj[:, par, :]

                def on(steps, name, tt=t):
                    dve.wait_ge(steps.sem, steps.at(tt, name))

                def step(name, ins, wait=True):
                    ins.then_inc(dve_s.sem, dve_s.one(name))
                    if wait:
                        on(dve_s, name)
                tt_, ts_ = nc.vector.tensor_tensor, nc.vector.tensor_scalar
                if t >= 1:
                    on(dve_s, "x2", t - 1)
                if 0 < t < PT:
                    step("halo", nc.vector.tensor_copy(cbuf[:, :, 0:HALO], cbuf[:, :, P:P + HALO]))
                else:
                    if t == PT:
                        dve.wait_ge(state_loaded, 32)
                    step("halo", nc.vector.tensor_copy(stat[:, 3:4], one))
                on(act_s, "expb")
                step("eb1", ts_(small[:, EB1, :], small[:, EB, :], 1.0, None, ALU.add))
                step("beta", nc.vector.reciprocal(small[:, BETA, :], small[:, EB1, :]))
                step("apre", tt_(small[:, APRE, :], pt[:, C_A:C_A + H_DN], dn_small[:, 1, :], ALU.add))
                step("aabs", nc.vector.scalar_tensor_tensor(small[:, AABS, :], small[:, APRE, :], -1.0,
                                                            small[:, APRE, :], ALU.mult, ALU.max))
                step("amax", ts_(small[:, AMAX, :], small[:, APRE, :], 0.0, None, ALU.max))
                on(act_s, "lnsp")
                step("sp", tt_(small[:, ASP, :], small[:, AMAX, :], small[:, SPL, :], ALU.add))
                step("g", tt_(small[:, G, :], small[:, ASP, :], dn_small[:, 3, :], ALU.mult))
                if t == PT:
                    nc.vector.memset(small[DEC:P, BETA, :], 0.0)
                    step("gz", nc.vector.memset(small[DEC:P, G, :], 0.0))
                else:
                    step("gz", nc.vector.tensor_copy(stat[:, 3:4], one))
                on(act_s, "cTc")
                for i in range(CONV_W):
                    for c in range(CONV_BLOCKS):
                        src = cbuf[:, c, i:i + P]
                        w = conv_w[:, c, i:i + 1]
                        if i == 0:
                            last = ts_(cy[:, c, :], src, w, None, ALU.mult)
                        else:
                            last = nc.vector.scalar_tensor_tensor(cy[:, c, :], src, w, cy[:, c, :], ALU.mult, ALU.add)
                    if i == 0:
                        step("conv0", last)
                    elif i < 3:
                        step(f"conv{i}", last)
                    else:
                        step("conv3", last)
                on(act_s, "sq")
                step("ssq", nc.vector.tensor_reduce(ssq[:, :], wide[:, :].rearrange("p (h d) -> p h d", d=DH), AX.X,
                                                    ALU.add))
                on(act_s, "rsq")
                step("qkn0", tt_(wide[:, :].rearrange("p (h d) -> p h d", d=DH),
                                 pt[:, 0:2 * AT_W].rearrange("p (h d) -> p h d", d=DH),
                                 rsq[:, :].unsqueeze(2).to_broadcast([P, 16, DH]), ALU.mult))
                if t > PT - PAST_TILES:
                    dve.wait_ge(k_kept, 16 * (t - PT + PAST_TILES))
                step("qkn", tt_(qkn[:, :], wide[:, :], head_gain[:, :], ALU.mult))
                on(pe_s, "gcol")
                step("gcol", nc.vector.tensor_copy(small[:, GCOL, :], X[:, 0:H_DN]))
                on(act_s, "growc")
                for h in range(H_DN):
                    last = ts_(dec[:, h, :], grow[:, h, :], small[:, GCOL, h:h + 1], 0.0, ALU.subtract, ALU.min)
                step("dif", last)
                step("glg", tt_(small[:, GLG, :], grow[:, :, P - 1], small[:, GCOL, :], ALU.subtract))
                on(act_s, "crs")
                step("qkd", tt_(qkd[:, :, :], cc[:, 0:8, :], csq[:, :, :], ALU.mult))
                step("decT", tt_(decT[:, :, :], dec[:, :, :], tri.unsqueeze(1).to_broadcast([P, 4, P]), ALU.mult))
                on(act_s, "browc")
                step("m1", tt_(m1[:, :, :], decT[:, :, :], brow[:, :, :], ALU.mult))
                step("bneg", ts_(small[:, BNEG, :], small[:, BETA, :], -1.0, None, ALU.mult))
                step("kscale", tt_(small[:, BNEG, :], small[:, BNEG, :], small[:, EGC, :], ALU.mult))
                on(pe_s, "kvT")
                for h in range(H_DN):
                    last = ts_(kbn[:, h, :], X3[:, h, :], small[:, BNEG, h:h + 1], None, ALU.mult)
                step("kbn", last)
                for h in range(H_DN):
                    last = ts_(kd[:, h, :], X3[:, h, :], small[:, EKD, h:h + 1], None, ALU.mult)
                step("kd", last)
                for h in range(H_DN):
                    last = ts_(vb[:, h, :], Y3[:, h, :], small[:, BETA, h:h + 1], None, ALU.mult)
                step("vb", last)
                step("qg", tt_(qg[:, :, :], qkd[:, 0:4, :], egrow[:, :, :], ALU.mult))
                on(pe_s, "kk")
                step("at0", tt_(m1[:, :, :], X3, m1[:, :, :], ALU.mult))
                step("AT", tt_(AT[:, :, :], m1[:, :, :],
                               cs[:, C_STRICT:C_STRICT + P].unsqueeze(1).to_broadcast([P, 4, P]), ALU.mult))
                step("QK", tt_(QK[:, :, :], Y3, decT[:, :, :], ALU.mult))
                on(pe_s, "A")
                step("T0", tt_(W[:, :, :], Z3, level(0), ALU.mult))
                step("T", tt_(T[:, :, :], ident4, W[:, :, :], ALU.subtract))
                step("Z0", tt_(W[:, :, :], AT[:, :, :], level(LEVELS), ALU.mult))
                step("Z", tt_(Z[:, :, :], ident4, W[:, :, :], ALU.subtract))
                for s in lv:
                    on(pe_s, f"w{s}")
                    step(f"W{s}", tt_(W[:, :, :], X3, level(s), ALU.mult))
                    on(pe_s, f"t{s}")
                    step(f"T{s}", tt_(T[:, :, :], T[:, :, :], Y3, ALU.subtract), False)
                    on(pe_s, f"z{s}")
                    step(f"Z{s}", tt_(Z[:, :, :], Z[:, :, :], Z3, ALU.subtract))
                on(pe_s, "ds")
                for h in range(H_DN):
                    last = nc.vector.scalar_tensor_tensor(S[:, h, :], S[:, h, :], egrow[:, h, P - 1:P], X3[:, h, :],
                                                          ALU.mult, ALU.add)
                step("S", last)
                on(act_s, "osq")
                step("ossq", nc.vector.tensor_reduce(small[:, OSS, :], osq[:, :, :], AX.X, ALU.add))
                on(act_s, "ors")
                step("oz", tt_(osq[:, :, :], oS[:, :, :], small[:, EB1, :].unsqueeze(2).to_broadcast([P, 4, P]),
                               ALU.mult))
                step("cat1", tt_(cat[:, AT_W:D].rearrange("p (h n) -> p h n", h=4), osq[:, :, :], zs[:, :, :],
                                 ALU.mult), False)
                slots, at = band(t)
                nk = len(slots) * P
                for h in range(H_AT):
                    on(pe_s, f"sc{h}")
                    if h >= 2:
                        on(act_s, f"exp{h - 2}")
                    step(f"sm{h}", nc.vector.tensor_tensor_reduce(
                        biased[:, h % 2, 0:nk], SC[:, 0:nk], bias[:, h, at:at + nk], 1.0, NEG, ALU.add, ALU.max,
                        top[:, h:h + 1]))
                    step(f"nt{h}", ts_(ntop[:, h:h + 1], top[:, h:h + 1], -1.0, None, ALU.mult), False)
                on(act_s, f"exp{H_AT - 1}")
                step("inv", nc.vector.reciprocal(inv[:, :], sums[:, :]))
                on(pe_s, f"pv{H_AT - 1}")
                step("ao", tt_(ao[:, :].rearrange("p (h d) -> p h d", d=DH), OB.ap().rearrange("p (h d) -> p h d", d=DH),
                               inv[:, :].unsqueeze(2).to_broadcast([P, H_AT, DH]), ALU.mult), False)
                on(pe_s, "catT")
                step("catT", tt_(catT[:, :, :], SC.ap().rearrange("p (k n) -> p k n", k=KD),
                                 cat_gain[:, :].unsqueeze(2).to_broadcast([P, KD, P]), ALU.mult), False)
                on(pe_s, "out")
                dve.wait_ge(x_loaded, 16 * (t + 1))
                step("x2", tt_(xt[:, :], xt[:, :], PTp.ap(), ALU.add))

        @block.tensor
        def _(pe):
            for t in range(NT):
                par = t % 2
                pt = pj[:, par, :]

                def on(steps, name, tt=t):
                    pe.wait_ge(steps.sem, steps.at(tt, name))

                def done(name, ins):
                    ins.then_inc(pe_s.sem, pe_s.one(name))
                mm, tr = nc.tensor.matmul, nc.tensor.transpose
                if t >= 1:
                    on(dve_s, "x2", t - 1)
                pe.wait_ge(pj_loaded[par], 16 * (t // 2 + 1))
                for c in range(CONV_BLOCKS):
                    last = tr((X3, Y3, Z3)[c // 4][:, c % 4, :], pt[:, C_DN + c * P:C_DN + (c + 1) * P], ident)
                done("convT", last)
                on(act_s, "cTc")
                on(dve_s, "gz")
                done("gcol", mm(X[:, 0:H_DN], tri, small[:, G, :], start=True, stop=True))
                for h in range(H_DN):
                    mm(Y3[:, h, :], small[:, G, h:h + 1].to_broadcast([P, P]), tri, start=True, stop=True)
                    last = mm(Z3[:, h, :], small[:, BETA, h:h + 1].to_broadcast([P, P]), ident, start=True, stop=True)
                done("rows", last)
                on(dve_s, "qkn")
                for c in range(8):
                    last = tr(SC[:, c * P:(c + 1) * P], qkn[:, c * P:(c + 1) * P], ident)
                done("qkT", last)
                if t == PT:
                    pe.wait_ge(past_loaded, 16 * 2 * PAST_TILES)
                    on(act_s, "qkTc")
                    for m in range(PAST_TILES):
                        if m >= 2:
                            pe.wait_ge(past_copied, m - 1)
                        for c in range(4):
                            last = tr(SC[:, (m % 2) * 512 + c * P:(m % 2) * 512 + (c + 1) * P],
                                      past_k[:, m, c * P:(c + 1) * P], ident)
                        last.then_inc(past_turned, 1)
                on(act_s, "csq")
                on(act_s, "browc")
                on(dve_s, "gcol")
                for n, b in enumerate((X, Y)):
                    last = mm(b[:, :], ones, csq[:, 4 * n:4 * n + 4, :].rearrange("p h n -> p (h n)"), start=True,
                              stop=True)
                done("norms", last)
                on(dve_s, "qkd")
                for h in range(H_DN):
                    tr(X3[:, h, :], qkd[:, 4 + h, :], ident)
                    last = tr(Y3[:, h, :], cc[:, 8 + h, :], ident)
                done("kvT", last)
                on(dve_s, "vb")
                for h in range(H_DN):
                    mm(X3[:, h, :], qkd[:, 4 + h, :], qkd[:, 4 + h, :], start=True, stop=True)
                    last = mm(Y3[:, h, :], qkd[:, 4 + h, :], qkd[:, h, :], start=True, stop=True)
                done("kk", last)
                on(dve_s, "AT")
                for h in range(H_DN):
                    last = tr(Z3[:, h, :], AT[:, h, :], ident)
                done("A", last)
                for s in lv:
                    on(dve_s, "Z" if s == 1 else f"Z{s - 1}")
                    for h in range(H_DN):
                        last = mm(X3[:, h, :], AT[:, h, :], T[:, h, :], start=True, stop=True)
                    done(f"w{s}", last)
                    on(dve_s, f"W{s}")
                    for h in range(H_DN):
                        last = mm(Y3[:, h, :], Z[:, h, :], W[:, h, :], start=True, stop=True)
                    done(f"t{s}", last)
                    for h in range(H_DN):
                        last = mm(Z3[:, h, :], W[:, h, :], Z[:, h, :], start=True, stop=True)
                    done(f"z{s}", last)
                on(dve_s, f"Z{lv[-1]}")
                for h in range(H_DN):
                    last = mm(X3[:, h, :], kbn[:, h, :], Z[:, h, :], start=True, stop=True)
                done("wT", last)
                on(act_s, "wTc")
                if t == PT:
                    pe.wait_ge(state_loaded, 32)
                for h in range(H_DN):
                    mm(Y3[:, h, :], Z[:, h, :], vb[:, h, :], start=True, stop=False)
                    last = mm(Y3[:, h, :], wT[:, h, :], S[:, h, :], start=False, stop=True)
                done("vn", last)
                on(act_s, "vnc")
                for h in range(H_DN):
                    mm(Z3[:, h, :], qg[:, h, :], S[:, h, :], start=True, stop=False)
                    last = mm(Z3[:, h, :], QK[:, h, :], vn[:, h, :], start=False, stop=True)
                done("o", last)
                for h in range(H_DN):
                    last = mm(X3[:, h, :], kd[:, h, :], vn[:, h, :], start=True, stop=True)
                done("ds", last)
                slots, at = band(t)
                on(act_s, "qkTc")
                if t == PT:
                    pe.wait_ge(past_copied, PAST_TILES)
                pe.wait_ge(vh_loaded, 16 * (t + 1))

                def scores(h):
                    if h >= 1:
                        on(dve_s, f"sm{h - 1}")
                    r = slice(DH * (h % 2), DH * (h % 2) + DH)
                    for n, s in enumerate(slots):
                        last = mm(SC[:, n * P:(n + 1) * P], qT[r, h // 2, :], kT[r, h // 2, s, :], start=True,
                                  stop=True)
                    done(f"sc{h}", last)
                for h in range(H_AT):
                    scores(h)
                    on(act_s, f"exp{h}")
                    if h >= 1:
                        on(act_s, f"ptc{h - 1}")
                    for n in range(len(slots)):
                        last = tr(PTp[:, n * P:(n + 1) * P], prob[:, h % 2, n * P:(n + 1) * P], ident)
                    done(f"pt{h}", last)
                    on(act_s, f"ptc{h}")
                    for n, s in enumerate(slots):
                        last = mm(OB[:, h * DH:(h + 1) * DH], probT[:, n * P:(n + 1) * P],
                                  vh[:, s, h * DH:(h + 1) * DH], start=(n == 0), stop=(n == len(slots) - 1))
                    done(f"pv{h}", last)
                on(act_s, "cat0")
                on(dve_s, "cat1")
                for k in range(KD):
                    last = tr(SC[:, k * P:(k + 1) * P], cat[:, k * P:(k + 1) * P], ident)
                done("catT", last)
                on(dve_s, "catT")
                for half in range(2):
                    for k in range(KD):
                        last = mm(PTp[:, half * 512:(half + 1) * 512], catT[:, k, :],
                                  w_out[:, k, half * 512:(half + 1) * 512], start=(k == 0), stop=(k == KD - 1))
                done("out", last)


IN_SHAPES = dict(
    x_prompt=(SEQ, D), x_sample=(DEC, D), cache_k=(WINDOW, AT_W), cache_v=(WINDOW, AT_W),
    conv_state=(P, CONV_BLOCKS, HALO), state=(H_DN, DK, DK), ln1=(P, KD), w_in=(D, IN_W),
    conv_w=(P, CONV_BLOCKS, CONV_W), a_log=(1, H_DN), dt_bias=(1, H_DN), dn_norm=(DK, 1), q_norm=(1, DH),
    k_norm=(1, DH), rel_bias=(H_AT, N_REL), attn_norm=(P, AT_W // P), w_out=(D, D), ln2=(P, KD),
    wq=(2 * PH, P, KD, P), keys=(P, 2 * PH, NK), u=(GROUPS, P, JG, KD, P), v=(GROUPS, P, JG, D), consts=(P, C_END))
OUT_SHAPES = dict(
    y_prompt=(SEQ, D), y_sample=(DEC, D), p_k=(WINDOW, AT_W), p_v=(WINDOW, AT_W), p_conv=(HALO, CONV_CH),
    p_state=(H_DN, DK, DK), s_k=(DEC, AT_W), s_v=(DEC, AT_W), s_conv=(HALO, CONV_CH), s_state=(H_DN, DK, DK))


def rows(prompt, sample):
    return lambda t: prompt[t * P:(t + 1) * P, :] if t < PT else sample


def layer(nc, I, O):
    proj = nc.dram_tensor("proj", [PADTOK, IN_W], F32, kind="Internal").ap()
    toeplitz = nc.dram_tensor("toeplitz", [H_AT, TOE], F32, kind="Internal").ap()
    x2 = nc.dram_tensor("x2", [TOK, D], F32, kind="Internal").ap()
    gates = nc.dram_tensor("gates", [GROUPS, P, NB, JG * GB], F32, kind="Internal").ap()
    x_tile = rows(I["x_prompt"], I["x_sample"])
    x2_tile = rows(x2, x2[SEQ:TOK, :])
    ident_d, eps_d = I["consts"][:, C_IDENT:C_IDENT + P], I["consts"][:, C_EPS:C_EPS + 1]
    iota_d = I["consts"][:, C_IOTA:C_IOTA + P]
    project(nc, x_tile, I["ln1"], I["w_in"], proj, ident_d, eps_d)
    mix(nc, I, proj, toeplitz, x_tile, x2_tile, O)
    with nc.sbuf_tensor("h2_hi", [P, KD, TOK], F32R) as h_hi, nc.sbuf_tensor("h2_lo", [P, KD, TOK], F32R) as h_lo:
        normed_transposed(nc, "n2", x2_tile, I["ln2"], h_hi, h_lo, ident_d, eps_d)
        with nc.sbuf_tensor("sel_i", [P, PADTOK], F32) as sel_i, nc.sbuf_tensor("sel_j", [P, PADTOK], F32) as sel_j, \
                nc.sbuf_tensor("sel_g", [P, PADTOK], F32) as sel_g:
            route(nc, h_hi, h_lo, I["wq"], I["keys"], ident_d, iota_d[:, 0:TOPK], sel_i, sel_j, sel_g)
            gate_matrices(nc, sel_i, sel_j, sel_g, iota_d, gates)
        experts(nc, h_hi, h_lo, gates, I["u"], I["v"], x2_tile, ident_d, rows(O["y_prompt"], O["y_sample"]))


def laid_out(inputs):
    a = {k: np.asarray(v)[0] for k, v in inputs.items()}

    def blocks(x):
        return x.reshape(-1, P).T
    return dict(
        x_prompt=a["x_prompt"], x_sample=a["x_sample"], cache_k=a["cache_attn_k"][0].reshape(WINDOW, AT_W),
        cache_v=a["cache_attn_v"][0].reshape(WINDOW, AT_W),
        conv_state=a["state_dn_conv"][0].reshape(HALO, CONV_BLOCKS, P).transpose(2, 1, 0), state=a["state_dn"][0],
        ln1=blocks(a["ln1"]), w_in=a["w_in"], conv_w=a["conv_w"].reshape(CONV_W, CONV_BLOCKS, P).transpose(2, 1, 0),
        a_log=a["a_log"][None], dt_bias=a["dt_bias"][None], dn_norm=a["dn_norm"][:, None], q_norm=a["q_norm"][None],
        k_norm=a["k_norm"][None], rel_bias=a["rel_bias"][:, ::-1], attn_norm=blocks(a["attn_norm"]),
        w_out=a["w_out"], ln2=blocks(a["ln2"]),
        wq=a["peer_wq"].reshape(KD, P, 2 * PH, P).transpose(2, 1, 0, 3),
        keys=a["peer_keys"].reshape(2 * PH, NK, P).transpose(2, 0, 1),
        u=a["peer_u"].reshape(NK, GROUPS, JG, KD, P).transpose(1, 4, 2, 3, 0),
        v=a["peer_v"].reshape(NK, GROUPS, JG, D).transpose(1, 0, 2, 3), consts=constants())


def kernel(**inputs):
    import concourse.bacc as bacc
    from concourse.bass_utils import run_bass_kernel_spmd

    arrays = {f"in_{k}": np.ascontiguousarray(v) for k, v in laid_out(inputs).items()}
    nc = bacc.Bacc("TRN2", target_bir_lowering=False, num_devices=1)
    I = {k: nc.dram_tensor(f"in_{k}", shape, F32, kind="ExternalInput").ap() for k, shape in IN_SHAPES.items()}
    O = {k: nc.dram_tensor(f"out_{k}", shape, F32, kind="ExternalOutput").ap() for k, shape in OUT_SHAPES.items()}
    layer(nc, I, O)
    r = run_bass_kernel_spmd(nc, [arrays], core_ids=[0]).results[0]
    o = {k: np.asarray(r[f"out_{k}"]) for k in OUT_SHAPES}
    return (o["y_prompt"][None], o["y_sample"][None],
            o["p_k"].reshape(1, 1, WINDOW, H_AT, DH), o["p_v"].reshape(1, 1, WINDOW, H_AT, DH),
            o["p_conv"][None, None], o["p_state"][None, None],
            o["s_k"].reshape(1, 1, DEC, H_AT, DH), o["s_v"].reshape(1, 1, DEC, H_AT, DH),
            o["s_conv"][None, None], o["s_state"][None, None])
```

```python
from contextlib import ExitStack, contextmanager

import numpy as np

import concourse.bass as bass
from concourse import mybir

F32 = mybir.dt.float32
F32R = mybir.dt.float32r
U32 = mybir.dt.uint32
ALU = mybir.AluOpType
ACT = mybir.ActivationFunctionType
AX = mybir.AxisListType

P = 128
D = 1024
KD = D // P
SEQ = 1024
DEC = 64
TOK = SEQ + DEC
PT = SEQ // P
NT = PT + 1
PADTOK = NT * P
CHUNK = 64
H_AT = 8
DH = 64
H_DN = 4
DK = 128
AT_W = H_AT * DH
DN_W = H_DN * DK
CONV_W = 4
HALO = CONV_W - 1
CONV_CH = 3 * DN_W
CONV_BLOCKS = CONV_CH // P
IN_W = 3 * AT_W + CONV_CH + DN_W + 2 * H_DN
C_AK, C_AV, C_DN, C_Z = AT_W, 2 * AT_W, 3 * AT_W, 3 * AT_W + CONV_CH
C_B = C_Z + DN_W
C_A = C_B + H_DN
WINDOW = 8 * CHUNK
PAST_TILES = WINDOW // P
BAND_TILES = PAST_TILES + 1
BAND = BAND_TILES * P
MAX_REL = 128
N_REL = 2 * MAX_REL + 1
PH = 8
NK = 128
TOPK = 16
EPS = 1e-6
NEG = -1e30
COLS = 450
TAIL = IN_W % COLS
FULL_BLOCKS = IN_W // COLS
LEVELS = 7
RING = 3


def rows_of(t):
    return P if t < PT else DEC


class Steps:

    def __init__(self, sem, names):
        self.sem, self.names, self.emitted = sem, list(names), 0

    def at(self, t, name):
        return t * len(self.names) + self.names.index(name) + 1

    def one(self, name):
        assert self.names[self.emitted % len(self.names)] == name, name
        self.emitted += 1
        return 1


def reach(eng, sem, value):
    if not (isinstance(value, int) and value <= 0):
        eng.wait_ge(sem, value)


def normed_transposed(nc, tag, source, gain, hi, lo, ident_d, eps_d, beside=None):
    names_act = ["square0"] + [x for t in range(NT) for x in
                               [f"log{t}"] + ([f"square{t + 1}"] if t + 1 < NT else []) + [f"rstd{t}", f"scaled{t}"]]
    names_dve = ["gained", "high", "low"]
    with ExitStack() as ctx:
        def sb(name, shape, dt=F32):
            return ctx.enter_context(nc.sbuf_tensor(f"{tag}_{name}", shape, dt))

        def sem(name):
            return ctx.enter_context(nc.semaphore(f"{tag}_{name}"))
        x = sb("x", [P, 3, D])
        junk = sb("junk", [P, D])
        xn = sb("xn", [P, 2, D])
        tmp = sb("tmp", [P, KD, P])
        stat = sb("stat", [P, 3, NT])
        ident = sb("ident", [P, P])
        gain_sb = sb("gain", [P, KD])
        eps = sb("eps", [P, 1])
        psum = ctx.enter_context(nc.psum_tensor(f"{tag}_turned", [P, 2, KD, P], F32))
        consts = sem("consts")
        x_loaded = [sem(f"x_loaded{i}") for i in range(3)]
        act_done = Steps(sem("act_done"), names_act)
        turned = sem("turned")
        dve_done = Steps(sem("dve_done"), names_dve)
        block = ctx.enter_context(nc.Block())

        @block.sync
        def _(sp):
            sp.dma_start(ident[:, :], ident_d).then_inc(consts, 16)
            sp.dma_start(gain_sb[:, :], gain).then_inc(consts, 16)
            with nc.allow_non_contiguous_dma("one number to a partition"):
                sp.dma_start(eps[:, :], eps_d).then_inc(consts, 16)
            for t in range(NT):
                if t >= 3:
                    sp.wait_ge(act_done.sem, act_done.at(0, f"scaled{t - 3}"))
                sp.dma_start(x[0:rows_of(t), t % 3, :], source(t)).then_inc(x_loaded[t % 3], 16)

        @block.scalar
        def _(act):
            nc.scalar.preload_act_table_set("natural_log_exp_and_others")
            act.wait_ge(consts, 48)

            def step(name, *args, **kw):
                nc.scalar.activation(*args, **kw).then_inc(act_done.sem, act_done.one(name))

            def square(t):
                n = rows_of(t)
                act.wait_ge(x_loaded[t % 3], 16 * (t // 3 + 1))
                if t >= 1:
                    act.wait_ge(act_done.sem, act_done.at(0, f"square{t - 1}"))
                step(f"square{t}", junk[0:n, :], x[0:n, t % 3, :], ACT.Square, accum_out=stat[0:n, 0, t:t + 1])

            square(0)
            for t in range(NT):
                n = rows_of(t)
                act.wait_ge(act_done.sem, act_done.at(0, f"square{t}"))
                step(f"log{t}", stat[0:n, 1, t:t + 1], stat[0:n, 0, t:t + 1], ACT.Ln, bias=eps[0:n, :], scale=1.0 / D)
                if t + 1 < NT:
                    square(t + 1)
                act.wait_ge(act_done.sem, act_done.at(0, f"log{t}"))
                step(f"rstd{t}", stat[0:n, 2, t:t + 1], stat[0:n, 1, t:t + 1], ACT.Exp, scale=-0.5)
                act.wait_ge(act_done.sem, act_done.at(0, f"rstd{t}"))
                if t >= 2:
                    act.wait_ge(turned, t - 1)
                step(f"scaled{t}", xn[0:n, t % 2, :], x[0:n, t % 3, :], ACT.Copy, scale=stat[0:n, 2, t:t + 1])

        if beside is not None:
            block.gpsimd(beside)

        @block.tensor
        def _(pe):
            pe.wait_ge(consts, 48)
            for t in range(NT):
                n = rows_of(t)
                pe.wait_ge(act_done.sem, act_done.at(0, f"scaled{t}"))
                if t >= 2:
                    pe.wait_ge(dve_done.sem, dve_done.at(t - 2, "gained"))
                for k in range(KD):
                    last = nc.tensor.transpose(psum[:, t % 2, k, 0:n], xn[0:n, t % 2, k * P:(k + 1) * P],
                                               ident[0:n, 0:n])
                last.then_inc(turned, 1)

        @block.vector
        def _(dve):
            if hi.shape[2] > TOK:
                nc.vector.memset(hi[:, :, TOK:].bitcast(F32), 0.0)
                nc.vector.memset(lo[:, :, TOK:].bitcast(F32), 0.0)
            dve.wait_ge(consts, 48)
            for t in range(NT):
                n = rows_of(t)
                cols = slice(t * P, t * P + n)
                dve.wait_ge(turned, t + 1)
                if t >= 1:
                    dve.wait_ge(dve_done.sem, dve_done.at(t - 1, "low"))
                nc.vector.tensor_tensor(tmp[:, :, 0:n], psum[:, t % 2, :, 0:n],
                                        gain_sb[:, :].unsqueeze(2).to_broadcast([P, KD, n]),
                                        ALU.mult).then_inc(dve_done.sem, 1)
                dve.wait_ge(dve_done.sem, dve_done.at(t, "gained"))
                nc.vector.tensor_copy(hi[:, :, cols], tmp[:, :, 0:n]).then_inc(dve_done.sem, 1)
                dve.wait_ge(dve_done.sem, dve_done.at(t, "high"))
                nc.vector.tensor_tensor(lo[:, :, cols], tmp[:, :, 0:n], hi[:, :, cols].bitcast(F32),
                                        ALU.subtract).then_inc(dve_done.sem, 1)


def project(nc, I, x_tile, proj, toeplitz, bias):
    w_in = I["w_in"]
    ident_d, eps_d = I["consts"][:, C_IDENT:C_IDENT + P], I["consts"][:, C_EPS:C_EPS + 1]
    with ExitStack() as ctx:
        h_hi = ctx.enter_context(nc.sbuf_tensor("h_hi", [P, KD, PADTOK], F32R))
        h_lo = ctx.enter_context(nc.sbuf_tensor("h_lo", [P, KD, PADTOK], F32R))
        w_raw = ctx.enter_context(nc.sbuf_tensor("pj_w_raw", [P, KD, COLS], F32))
        w_first = ctx.enter_context(nc.semaphore("pj_w_first"))
        w_view = w_in.rearrange("(k p) n -> p k n", p=P)
        with relative_bias_loads(nc, I, toeplitz) as (loads, finish):
            def beside(pool):
                loads(pool)
                pool.dma_start(w_raw[:, :, :], w_view[:, :, 0:COLS]).then_inc(w_first, 16)
                pool.wait_ge(w_first, 16)
            normed_transposed(nc, "n1", x_tile, I["ln1"], h_hi, h_lo, ident_d, eps_d, beside)
            finish(bias)

        def sb(name, shape, dt=F32):
            return ctx.enter_context(nc.sbuf_tensor(f"pj_{name}", shape, dt))

        def sem(name):
            return ctx.enter_context(nc.semaphore(f"pj_{name}"))
        w_hi = sb("w_hi", [P, 2, KD, COLS], F32R)
        w_lo = sb("w_lo", [P, 2, KD, COLS], F32R)
        out = sb("out", [P, RING, COLS])
        psum = ctx.enter_context(nc.psum_tensor("pj_acc", [P, 4, 512], F32))
        w_loaded, w_high, w_low = sem("w_loaded"), sem("w_high"), sem("w_low")
        products, copied = sem("products"), sem("copied")
        stored = [sem(f"stored{i}") for i in range(RING)]
        blocks = FULL_BLOCKS + 1

        def width(cb):
            return TAIL if isinstance(cb, int) and cb == FULL_BLOCKS else COLS

        def each_block(eng, body):
            body(0, 0)
            body(1, 1)
            with eng.Fori(1, FULL_BLOCKS // 2) as i:
                body(i * 2, 0)
                body(i * 2 + 1, 1)
            for cb in range(FULL_BLOCKS // 2 * 2, blocks):
                body(cb, cb % 2)

        block = ctx.enter_context(nc.Block())

        @block.sync
        def _(sp):
            def load(cb):
                w = width(cb)
                start = cb * COLS
                sp.dma_start(w_raw[:, :, 0:w], w_view[:, :, bass.ds(start, w)]).then_inc(w_loaded, 16)

            def body(cb, par):
                if not (isinstance(cb, int) and cb == blocks - 1):
                    sp.wait_ge(w_high, cb + 1)
                    sp.wait_ge(w_low, cb + 1)
                    load(cb + 1)
                w = width(cb)
                for t in range(NT):
                    sp.wait_ge(copied, cb * NT + t + 1)
                    sp.dma_start(proj[t * P:(t + 1) * P, bass.ds(cb * COLS, w)],
                                 out[:, t % RING, 0:w]).then_inc(stored[t % RING], 16)
            each_block(sp, body)
            for s in stored:
                sp.wait_ge(s, 16 * (NT // RING) * blocks)

        @block.scalar
        def _(act):
            act.wait_ge(w_first, 16)
            nc.scalar.activation(w_hi[:, 0, :, :], w_raw[:, :, :], ACT.Copy).then_inc(w_high, 1)

            def body(cb, par):
                if not (isinstance(cb, int) and cb == blocks - 1):
                    reach(act, products, cb * NT)
                    nxt = cb + 1
                    w = width(nxt)
                    act.wait_ge(w_loaded, cb * 16 + 16)
                    nc.scalar.activation(w_hi[:, 1 - par, :, 0:w], w_raw[:, :, 0:w], ACT.Copy).then_inc(w_high, 1)
                w = width(cb)
                for t in range(NT):
                    act.wait_ge(products, cb * NT + t + 1)
                    reach(act, stored[t % RING], (cb * (NT // RING) + t // RING) * 16)
                    nc.scalar.activation(out[:, t % RING, 0:w], psum[:, t % 4, 0:w], ACT.Copy).then_inc(copied, 1)
            each_block(act, body)

        @block.vector
        def _(dve):
            dve.wait_ge(w_high, 1)
            nc.vector.tensor_tensor(w_lo[:, 0, :, :], w_raw[:, :, :], w_hi[:, 0, :, :].bitcast(F32),
                                    ALU.subtract).then_inc(w_low, 1)

            def body(cb, par):
                if not (isinstance(cb, int) and cb == blocks - 1):
                    w = width(cb + 1)
                    dve.wait_ge(w_high, cb + 2)
                    nc.vector.tensor_tensor(w_lo[:, 1 - par, :, 0:w], w_raw[:, :, 0:w],
                                            w_hi[:, 1 - par, :, 0:w].bitcast(F32), ALU.subtract).then_inc(w_low, 1)
            each_block(dve, body)

        @block.tensor
        def _(pe):
            def body(cb, par):
                w = width(cb)
                pe.wait_ge(w_low, cb + 1)
                for t in range(NT):
                    if t >= 4:
                        pe.wait_ge(copied, cb * NT + t - 3)
                    else:
                        reach(pe, copied, cb * NT)
                    cols = slice(t * P, (t + 1) * P)
                    n = 0
                    for a, b in ((h_hi, w_hi), (h_lo, w_hi), (h_hi, w_lo)):
                        for k in range(KD):
                            last = nc.tensor.matmul(psum[:, t % 4, 0:w], a[:, k, cols], b[:, par, k, 0:w],
                                                    start=(n == 0), stop=(n == 3 * KD - 1))
                            n += 1
                    last.then_inc(products, 1)
            each_block(pe, body)


CHUNKS = ((0, 384), (384, 384), (768, TOK - 768))
CW = 384
WIDTHS = [TOPK // (a + 1) for a in range(TOPK)]
STARTS = [sum(WIDTHS[:a]) for a in range(TOPK)]
N_CAND = sum(WIDTHS)
ROW_GROUPS = [(a, next((b for b in range(a, TOPK) if WIDTHS[b] != WIDTHS[a]), TOPK)) for a in range(TOPK)
              if a == 0 or WIDTHS[a] != WIDTHS[a - 1]]


def route(nc, h_hi, h_lo, wq, keys, ident_d, iota_d, starts_d, sel_i, sel_j, sel_g):
    with ExitStack() as ctx:
        def sb(name, shape, dt=F32):
            return ctx.enter_context(nc.sbuf_tensor(f"rt_{name}", shape, dt))

        def sem(name):
            return ctx.enter_context(nc.semaphore(f"rt_{name}"))
        w_raw = sb("w_raw", [P, 2, KD, P])
        w_hi = sb("w_hi", [P, 2, KD, P], F32R)
        w_lo = sb("w_lo", [P, 2, KD, P], F32R)
        keys_sb = sb("keys", [P, 2 * PH, NK])
        ident = sb("ident", [P, P])
        iota = sb("iota", [P, TOPK])
        query = sb("query", [P, PADTOK])
        score = sb("score", [P, 2, NT, NK])
        rest = sb("rest", [P, NT, NK])
        top_v = sb("top_v", [P, 2, NT, TOPK])
        top_i = sb("top_i", [P, 2, NT, TOPK], U32)
        top_f = sb("top_f", [P, 2, NT, TOPK])
        starts, starts_nk = sb("starts", [P, TOPK]), sb("starts_nk", [P, TOPK])
        cand, cand2 = sb("cand", [P, NT, N_CAND]), sb("cand2", [P, NT, N_CAND])
        cand_v = sb("cand_v", [P, NT, TOPK])
        cand_i = sb("cand_i", [P, NT, TOPK], U32)
        place_f = sb("place_f", [P, NT, TOPK])
        coded, rise = sb("coded", [P, NT, TOPK]), sb("rise", [P, NT, TOPK])
        code, start_f, second = sb("code", [P, NT, TOPK]), sb("start_f", [P, NT, TOPK]), sb("second", [P, NT, TOPK])
        code_i, start_i, key_i = (sb(n, [P, NT, TOPK], U32) for n in ("code_i", "start_i", "key_i"))
        hot = sb("hot", [P, 2, NT, TOPK, TOPK])
        less = sb("less", [P, NT, TOPK])
        expd = sb("expd", [P, NT, TOPK])
        total = sb("total", [P, 2, NT])
        chosen = sb("chosen", [P, 3, NT, PH * TOPK])
        qp = ctx.enter_context(nc.psum_tensor("rt_qp", [P, 3, 512], F32))
        sp_ = ctx.enter_context(nc.psum_tensor("rt_sp", [P, 3, 4, NK], F32))
        consts, cleared, w_loaded = sem("consts"), sem("cleared"), [sem("w_loaded0"), sem("w_loaded1")]
        w_high, w_low, queried, query_out = sem("w_high"), sem("w_low"), sem("queried"), sem("query_out")
        scored, score_out = sem("scored"), sem("score_out")
        top = Steps(sem("top"), ["first8", "rest", "first8_i", "next8", "next8_i"])
        pick_names = ["float", "coded", "rise", "sums", "first8", "rest", "first8_i", "next8", "next8_i", "place_f",
                      "less", "stairs"]
        pick = Steps(sem("pick"), pick_names)
        look = Steps(sem("look"), ["code", "code_i", "start_i", "key_i", "key", "start_f", "second", "hot"])
        final = Steps(sem("final"), ["total", "inv", "gate"])
        exps, looked_up, key_sum = sem("exps"), sem("looked_up"), sem("key_sum")
        sel_turned, sel_out = sem("sel_turned"), sem("sel_out")
        block = ctx.enter_context(nc.Block())

        @block.sync
        def _(sp):
            sp.dma_start(keys_sb[:, :, :], keys).then_inc(consts, 16)
            sp.dma_start(ident[:, :], ident_d).then_inc(consts, 16)
            sp.dma_start(iota[:, :], iota_d).then_inc(consts, 16)
            sp.dma_start(starts[:, :], starts_d).then_inc(consts, 16)
            for p in range(2):
                sp.dma_start(w_raw[:, p, :, :], wq[p]).then_inc(w_loaded[p], 16)
            with sp.Fori(1, PH) as h:
                for p in range(2):
                    sp.wait_ge(w_high, h * 2 + p - 1)
                    sp.wait_ge(w_low, h * 2 + p - 1)
                    sp.dma_start(w_raw[:, p, :, :], wq[h * 2 + p]).then_inc(w_loaded[p], 16)

        @block.scalar
        def _(act):
            act.wait_ge(cleared, 1)
            nc.scalar.preload_act_table_set("exp_and_others")

            def high(hp, h, p):
                act.wait_ge(w_loaded[p], h * 16 + 16)
                reach(act, queried, hp - 1)
                nc.scalar.activation(w_hi[:, p, :, :], w_raw[:, p, :, :], ACT.Copy).then_inc(w_high, 1)

            def exps_of(h):
                act.wait_ge(pick.sem, pick.at(h, "less"))
                nc.scalar.activation(expd[:, :, :], less[:, :, :], ACT.Exp).then_inc(exps, 1)

            def body(h, first, last_head):
                for p in range(2):
                    hp = h * 2 + p
                    if p == 0:
                        high(hp + 1, h, 1)
                    elif not last_head:
                        high(hp + 1, h + 1, 0)
                    act.wait_ge(queried, hp + 1)
                    reach(act, scored, hp)
                    for c, (at, n) in enumerate(CHUNKS):
                        last = nc.scalar.activation(query[:, at:at + n], qp[:, c, 0:n], ACT.Copy)
                    last.then_inc(query_out, 1)
                    act.wait_ge(scored, hp + 1)
                    if not first:
                        act.wait_ge(top.sem, top.at(hp - 2, "first8_i"))
                    for c in range(3):
                        n = min(4, NT - 4 * c)
                        last = nc.scalar.activation(score[:, p, 4 * c:4 * c + n, :], sp_[:, c, 0:n, :], ACT.Copy)
                    last.then_inc(score_out, 1)
                if not first:
                    exps_of(h - 1)
            high(0, 0, 0)
            body(0, True, False)
            with act.Fori(1, PH - 1) as h:
                body(h, False, False)
            body(PH - 1, False, True)
            exps_of(PH - 1)
            for s, dst in enumerate((sel_i, sel_j, sel_g)):
                act.wait_ge(sel_turned, s + 1)
                for c in range(3):
                    n = min(4, NT - 4 * c)
                    last = nc.scalar.activation(dst[:, 4 * c * P:(4 * c + n) * P],
                                                (qp if s % 2 == 0 else sp_.ap().rearrange("p c a b -> p c (a b)"))
                                                [:, c, 0:n * P], ACT.Copy)
                last.then_inc(sel_out, 1)

        @block.tensor
        def _(pe):
            pe.wait_ge(consts, 64)

            def body(h, first):
                for p in range(2):
                    hp = h * 2 + p
                    pe.wait_ge(w_low, hp + 1)
                    if not (first and p == 0):
                        pe.wait_ge(query_out, hp)
                    for c, (at, n) in enumerate(CHUNKS):
                        m = 0
                        for a, b in ((w_hi, h_hi), (w_hi, h_lo), (w_lo, h_hi)):
                            for k in range(KD):
                                last = nc.tensor.matmul(qp[:, c, 0:n], a[:, p, k, :], b[:, k, at:at + n],
                                                        start=(m == 0), stop=(m == 3 * KD - 1))
                                m += 1
                    last.then_inc(queried, 1)
                    pe.wait_ge(query_out, hp + 1)
                    if not (first and p == 0):
                        pe.wait_ge(score_out, hp)
                    for t in range(NT):
                        last = nc.tensor.matmul(sp_[:, t // 4, t % 4, :], query[:, t * P:(t + 1) * P],
                                                keys_sb[:, hp, :] if isinstance(hp, int) else
                                                keys_sb[:, bass.ds(hp, 1), :], start=True, stop=True)
                    last.then_inc(scored, 1)
            body(0, True)
            with pe.Fori(1, PH) as h:
                body(h, False)
            pe.wait_ge(final.sem, final.at(PH - 1, "gate"))
            pe.wait_ge(look.sem, look.at(PH - 1, "key"))
            pe.wait_ge(key_sum, PH)
            pe.wait_ge(score_out, 2 * PH)
            for s in range(3):
                if s == 2:
                    pe.wait_ge(sel_out, 1)
                for t in range(NT):
                    bank = (qp[:, t // 4, (t % 4) * P:(t % 4 + 1) * P] if s % 2 == 0 else sp_[:, t // 4, t % 4, :])
                    last = nc.tensor.transpose(bank, chosen[:, s, t, :], ident[:, :])
                last.then_inc(sel_turned, 1)

        @block.vector
        def _(dve):
            nc.vector.memset(query[:, TOK:PADTOK], 0.0).then_inc(cleared, 1)
            dve.wait_ge(consts, 64)

            def bc4(ap, dim):
                return ap.unsqueeze(dim).to_broadcast([P, NT, TOPK, TOPK])

            each_place = iota[:, :].unsqueeze(1).unsqueeze(1).to_broadcast([P, NT, TOPK, TOPK])
            nc.vector.tensor_scalar(starts_nk[:, :], starts[:, :], float(NK), None, ALU.mult).then_inc(cleared, 1)
            dve.wait_ge(cleared, 2)
            starts128 = starts_nk[:, :].unsqueeze(1).to_broadcast([P, NT, TOPK])

            def gates_of(h):
                dve.wait_ge(exps, h + 1)
                for name, ins in (
                        ("total", lambda: nc.vector.tensor_reduce(total[:, 0, :], expd[:, :, :], AX.X, ALU.add)),
                        ("inv", lambda: nc.vector.reciprocal(total[:, 1, :], total[:, 0, :])),
                        ("gate", lambda: nc.vector.tensor_tensor(
                            chosen[:, 2, :, bass.ds(h * TOPK, TOPK)], expd[:, :, :],
                            total[:, 1, :].unsqueeze(2).to_broadcast([P, NT, TOPK]), ALU.mult))):
                    ins().then_inc(final.sem, 1)
                    dve.wait_ge(final.sem, final.at(h, name))

            def first_keys_of(h):
                def step(name, ins):
                    ins.then_inc(look.sem, 1)
                    dve.wait_ge(look.sem, look.at(h, name))
                dve.wait_ge(looked_up, 2 * h + 1)
                step("code", nc.vector.tensor_reduce(code[:, :, :], hot[:, 0, :, :, :], AX.X, ALU.add))
                step("code_i", nc.vector.tensor_copy(code_i[:, :, :], code[:, :, :]))
                step("start_i", nc.vector.tensor_scalar(start_i[:, :, :], code_i[:, :, :], 7, None,
                                                        ALU.logical_shift_right))
                step("key_i", nc.vector.tensor_scalar(key_i[:, :, :], code_i[:, :, :], NK - 1, None, ALU.bitwise_and))
                step("key", nc.vector.tensor_copy(chosen[:, 0, :, bass.ds(h * TOPK, TOPK)], key_i[:, :, :]))
                step("start_f", nc.vector.tensor_copy(start_f[:, :, :], start_i[:, :, :]))
                step("second", nc.vector.tensor_tensor(second[:, :, :], place_f[:, :, :], start_f[:, :, :],
                                                       ALU.subtract))
                step("hot", nc.vector.tensor_tensor(hot[:, 1, :, :, :], bc4(second[:, :, :], 3), each_place,
                                                    ALU.is_equal))

            def second_keys_of(h):
                dve.wait_ge(looked_up, 2 * h + 2)
                nc.vector.tensor_reduce(chosen[:, 1, :, bass.ds(h * TOPK, TOPK)], hot[:, 1, :, :, :],
                                        AX.X, ALU.add).then_inc(key_sum, 1)

            def body(h, first):
                for p in range(2):
                    hp = h * 2 + p
                    dve.wait_ge(score_out, hp + 1)
                    if not first and p == 1:
                        first_keys_of(h - 1)
                    for t in range(NT):
                        last = nc.vector.max(top_v[:, p, t, 0:8], score[:, p, t, :])
                    last.then_inc(top.sem, 1)
                    dve.wait_ge(top.sem, top.at(hp, "first8"))
                    for t in range(NT):
                        last = nc.vector.match_replace(rest[:, t, :], top_v[:, p, t, 0:8], score[:, p, t, :], NEG)
                    last.then_inc(top.sem, 1)
                    for t in range(NT):
                        last = nc.vector.max_index(top_i[:, p, t, 0:8], top_v[:, p, t, 0:8], score[:, p, t, :])
                    last.then_inc(top.sem, 1)
                    dve.wait_ge(top.sem, top.at(hp, "rest"))
                    for t in range(NT):
                        last = nc.vector.max(top_v[:, p, t, 8:16], rest[:, t, :])
                    last.then_inc(top.sem, 1)
                    dve.wait_ge(top.sem, top.at(hp, "next8"))
                    for t in range(NT):
                        last = nc.vector.max_index(top_i[:, p, t, 8:16], top_v[:, p, t, 8:16], rest[:, t, :])
                    last.then_inc(top.sem, 1)
                    dve.wait_ge(top.sem, top.at(hp, "next8_i"))

                def step(name, ins, wait=True):
                    ins.then_inc(pick.sem, 1)
                    if wait:
                        dve.wait_ge(pick.sem, pick.at(h, name))

                if not first:
                    gates_of(h - 1)
                    second_keys_of(h - 1)
                step("float", nc.vector.tensor_copy(top_f[:, :, :, :], top_i[:, :, :, :]))
                step("coded", nc.vector.tensor_tensor(coded[:, :, :], top_f[:, 0, :, :], starts128, ALU.add))
                nc.vector.tensor_copy(rise[:, :, 0:1], coded[:, :, 0:1])
                step("rise", nc.vector.tensor_tensor(rise[:, :, 1:], coded[:, :, 1:], coded[:, :, 0:TOPK - 1],
                                                     ALU.subtract), False)
                for a, b in ROW_GROUPS:
                    w = WIDTHS[a]
                    last = nc.vector.tensor_tensor(
                        cand[:, :, STARTS[a]:STARTS[a] + (b - a) * w].rearrange("p t (a b) -> p t a b", b=w),
                        top_v[:, 0, :, a:b].unsqueeze(3).to_broadcast([P, NT, b - a, w]),
                        top_v[:, 1, :, 0:w].unsqueeze(2).to_broadcast([P, NT, b - a, w]), ALU.add)
                step("sums", last)
                for t in range(NT):
                    last = nc.vector.max(cand_v[:, t, 0:8], cand[:, t, :])
                step("first8", last)
                for t in range(NT):
                    last = nc.vector.match_replace(cand2[:, t, :], cand_v[:, t, 0:8], cand[:, t, :], NEG)
                step("rest", last)
                for t in range(NT):
                    last = nc.vector.max_index(cand_i[:, t, 0:8], cand_v[:, t, 0:8], cand[:, t, :])
                step("first8_i", last)
                for t in range(NT):
                    last = nc.vector.max(cand_v[:, t, 8:16], cand2[:, t, :])
                step("next8", last)
                for t in range(NT):
                    last = nc.vector.max_index(cand_i[:, t, 8:16], cand_v[:, t, 8:16], cand2[:, t, :])
                step("next8_i", last)
                step("place_f", nc.vector.tensor_copy(place_f[:, :, :], cand_i[:, :, :]))
                step("less", nc.vector.tensor_tensor(less[:, :, :], cand_v[:, :, :],
                                                     cand_v[:, :, 0:1].to_broadcast([P, NT, TOPK]), ALU.subtract),
                     False)
                step("stairs", nc.vector.tensor_tensor(
                    hot[:, 0, :, :, :], bc4(place_f[:, :, :], 3),
                    starts[:, :].unsqueeze(1).unsqueeze(1).to_broadcast([P, NT, TOPK, TOPK]), ALU.is_ge), False)
            for h in range(PH):
                body(h, h == 0)
            first_keys_of(PH - 1)
            gates_of(PH - 1)
            second_keys_of(PH - 1)
            dve.wait_ge(sel_out, 3)

        @block.gpsimd
        def _(pool):
            def low(hp, p):
                pool.wait_ge(w_high, hp + 1)
                reach(pool, queried, hp - 1)
                nc.gpsimd.tensor_tensor(w_lo[:, p, :, :], w_raw[:, p, :, :], w_hi[:, p, :, :].bitcast(F32),
                                        ALU.subtract).then_inc(w_low, 1)

            def look_up(h, q, steps, name):
                pool.wait_ge(steps.sem, steps.at(h, name))
                values = rise[:, :, :] if q == 0 else top_f[:, 1, :, :]
                nc.gpsimd.tensor_tensor(hot[:, q, :, :, :], hot[:, q, :, :, :],
                                        values.unsqueeze(2).to_broadcast([P, NT, TOPK, TOPK]),
                                        ALU.mult).then_inc(looked_up, 1)

            def body(h, blocks_left):
                look_up(h, 0, pick, "stairs")
                if blocks_left:
                    for p in range(2):
                        low(h * 2 + 4 + p, p)
                look_up(h, 1, look, "hot")
            for hp in range(4):
                low(hp, hp % 2)
            with pool.Fori(0, PH - 2) as h:
                body(h, True)
            body(PH - 2, False)
            body(PH - 1, False)


GB = 64
NB = TOK // GB
JG = 2
GROUPS = NK // JG
OH = 16
ON_ACT = 3


def gate_matrices(nc, sel_i, sel_j, sel_g, iota128_d, gates):
    with ExitStack() as ctx:
        def sb(name, shape, dt=F32):
            return ctx.enter_context(nc.sbuf_tensor(f"gt_{name}", shape, dt))

        def sem(name):
            return ctx.enter_context(nc.semaphore(f"gt_{name}"))
        iota = sb("iota", [P, NK])
        one_i = sb("one_i", [P, OH, NK])
        hot_j = sb("hot_j", [P, OH, NK])
        gate_j = sb("gate_j", [P, OH, NK])
        minus_i = sb("minus_i", [P, 2, GB])
        distance = sb("distance", [P, 4, NK])
        one = sb("one", [P, 1])
        negated, measured, compared_a = sem("negated"), sem("measured"), sem("compared_a")
        out = [sb("out0", [P, NK, GB]), sb("out1", [P, NK, GB])]
        psum = ctx.enter_context(nc.psum_tensor("gt_psum", [P, 4, 4, NK], F32))
        consts, compared_i, compared_j, gated = sem("consts"), sem("compared_i"), sem("compared_j"), sem("gated")
        multiplied, copied = sem("multiplied"), sem("copied")
        stored = [sem("stored0"), sem("stored1")]
        Q = GB // 4
        block = ctx.enter_context(nc.Block())

        def pairs(eng, body):
            body(0, 0, 0)
            body(1, 1, 0)
            with eng.Fori(1, NB // 2) as k:
                body(k * 2, 0, k)
                body(k * 2 + 1, 1, k)
            body(NB - 1, 0, NB // 2)

        @block.sync
        def _(sp):
            sp.dma_start(iota[:, :], iota128_d).then_inc(consts, 16)

            def body(b, slot, before):
                sp.wait_ge(copied, b * Q + Q)
                sp.dma_start(gates[:, :, bass.ds(b, 1), :].rearrange("g i b x -> i g (b x)"),
                             out[slot][:, :, :].rearrange("p (g j) t -> p g (j t)", j=JG)).then_inc(stored[slot], 16)
            pairs(sp, body)
            sp.wait_ge(stored[0], 16 * (NB // 2 + 1))
            sp.wait_ge(stored[1], 16 * (NB // 2))

        def spread(keys, b, q):
            return keys[:, bass.ds(b * GB + 4 * q, 4)].unsqueeze(2).to_broadcast([P, 4, NK])

        @block.vector
        def _(dve):
            dve.wait_ge(consts, 16)
            each_key = iota[:, :].unsqueeze(1).to_broadcast([P, 4, NK])
            nc.vector.memset(one[:, :], 1.0)

            def body(b, slot, before):
                first = isinstance(b, int) and b == 0
                nc.vector.tensor_scalar(minus_i[:, slot, :], sel_i[:, bass.ds(b * GB, GB)], -1.0, None,
                                        ALU.mult).then_inc(negated, 1)
                for q in range(Q):
                    s = (4 * q) % OH
                    if not (first and q < OH // 4):
                        dve.wait_ge(multiplied, b * Q + q + 1 - OH // 4)
                    nc.vector.tensor_tensor(hot_j[:, s:s + 4, :], each_key, spread(sel_j, b, q),
                                            ALU.is_equal).then_inc(compared_j, 1)
                    if q % 4 != ON_ACT:
                        nc.vector.tensor_tensor(one_i[:, s:s + 4, :], each_key, spread(sel_i, b, q),
                                                ALU.is_equal).then_inc(compared_i, 1)
            pairs(dve, body)

        @block.gpsimd
        def _(pool):
            def body(b, first):
                for q in range(Q):
                    s = (4 * q) % OH
                    if not (first and q < OH // 4):
                        pool.wait_ge(multiplied, b * Q + q + 1 - OH // 4)
                    pool.wait_ge(compared_j, b * Q + q + 1)
                    nc.gpsimd.tensor_tensor(gate_j[:, s:s + 4, :], hot_j[:, s:s + 4, :], spread(sel_g, b, q),
                                            ALU.mult).then_inc(gated, 1)
            body(0, True)
            with pool.Fori(1, NB) as b:
                body(b, False)

        @block.tensor
        def _(pe):
            def body(b, first):
                for q in range(Q):
                    if q % 4 == ON_ACT:
                        pe.wait_ge(compared_a, b * (Q // 4) + q // 4 + 1)
                    else:
                        pe.wait_ge(compared_i, b * (Q - Q // 4) + q - (q + 3 - ON_ACT) // 4 + 1)
                    pe.wait_ge(gated, b * Q + q + 1)
                    if not (first and q < 4):
                        pe.wait_ge(copied, b * Q + q - 3)
                    for r in range(4):
                        s = (4 * q + r) % OH
                        last = nc.tensor.matmul(psum[:, q % 4, r, :], one_i[:, s, :], gate_j[:, s, :],
                                                start=True, stop=True)
                    last.then_inc(multiplied, 1)
            body(0, True)
            with pe.Fori(1, NB) as b:
                body(b, False)

        @block.scalar
        def _(act):
            act.wait_ge(consts, 16)

            def body(b, slot, before):
                reach(act, stored[slot], before * 16)
                for q in range(Q):
                    if q % 4 == 0:
                        act.wait_ge(negated, b + 1)
                        reach(act, multiplied, b * Q + q)
                        reach(act, compared_a, b * (Q // 4) + q // 4)
                        s = 4 * ON_ACT
                        for r in range(4):
                            tok = 4 * (q + ON_ACT) + r
                            last = nc.scalar.activation(distance[:, r, :], iota[:, :], ACT.Square,
                                                        bias=minus_i[:, slot, tok:tok + 1])
                        last.then_inc(measured, 1)
                        act.wait_ge(measured, b * (Q // 4) + q // 4 + 1)
                        nc.scalar.activation(one_i[:, s:s + 4, :], distance[:, :, :], ACT.Relu, scale=-1.0,
                                             bias=one[:, :]).then_inc(compared_a, 1)
                    act.wait_ge(multiplied, b * Q + q + 1)
                    nc.scalar.activation(out[slot][:, :, 4 * q:4 * q + 4],
                                         psum[:, q % 4, :, :].rearrange("p t j -> p j t"), ACT.Copy).then_inc(copied, 1)
            pairs(act, body)


def experts(nc, h_hi, h_lo, gates, u, v, x2, ident_d, y_rows):
    NU = JG * len(CHUNKS)
    NV = len(CHUNKS) * KD
    VB = 5
    XR = 4
    with ExitStack() as ctx:
        def sb(name, shape, dt=F32):
            return ctx.enter_context(nc.sbuf_tensor(f"ex_{name}", shape, dt))

        def sem(name):
            return ctx.enter_context(nc.semaphore(f"ex_{name}"))
        y = sb("y", [P, KD, TOK])
        u_raw = sb("u_raw", [P, JG, KD, P])
        v_raw = sb("v_raw", [P, JG, D])
        u_hi, u_lo = sb("u_hi", [P, JG, KD, P], F32R), sb("u_lo", [P, JG, KD, P], F32R)
        v_hi, v_lo = sb("v_hi", [P, JG, D], F32R), sb("v_lo", [P, JG, D], F32R)
        gate = sb("gate", [P, NB, JG, GB])
        act_f = sb("act_f", [P, 2, CW])
        gated_f = sb("gated_f", [P, 2, CW])
        a_hi, a_lo = sb("a_hi", [P, JG, TOK], F32R), sb("a_lo", [P, JG, TOK], F32R)
        psum_u = ctx.enter_context(nc.psum_tensor("ex_psum_u", [P, 3, 512], F32))
        psum_v = ctx.enter_context(nc.psum_tensor("ex_psum_v", [P, VB, 512], F32))
        u_loaded, v_loaded, gate_loaded = sem("u_loaded"), sem("v_loaded"), sem("gate_loaded")
        u_high, u_low, v_high, v_low = sem("u_high"), sem("u_low"), sem("v_high"), sem("v_low")
        cleared, hidden, active, gated, a_high, a_low = (sem("cleared"), sem("hidden"), sem("active"), sem("gated"),
                                                         sem("a_high"), sem("a_low"))
        summed, added = sem("summed"), sem("added")
        units = [(j, c) for j in range(JG) for c in range(len(CHUNKS))]

        ident = sb("ident", [P, P])
        x = sb("x", [P, XR, D])
        id_loaded, x_loaded = sem("id_loaded"), [sem(f"x_loaded{i}") for i in range(XR)]

        def load_x(sp, t):
            if t >= XR:
                sp.wait_ge(stored[t % XR], 16 * (t // XR))
            sp.dma_start(x[0:rows_of(t), t % XR, :], x2(t)).then_inc(x_loaded[t % XR], 16)

        with nc.Block() as block:
            @block.sync
            def _(sp):
                sp.dma_start(u_raw[:, :, :, :], u[0]).then_inc(u_loaded, 16)

                def body(g, last):
                    reach(sp, gated, g * NU)
                    sp.dma_start(gate[:, :, :, :].rearrange("p b j t -> p b (j t)"), gates[g]).then_inc(gate_loaded, 16)
                    reach(sp, v_high, g)
                    reach(sp, v_low, g)
                    sp.dma_start(v_raw[:, :, :], v[g]).then_inc(v_loaded, 16)
                    if not last:
                        sp.wait_ge(u_high, g + 1)
                        sp.wait_ge(u_low, g + 1)
                        sp.dma_start(u_raw[:, :, :, :], u[g + 1]).then_inc(u_loaded, 16)
                body(0, False)
                with sp.Fori(1, GROUPS - 1) as g:
                    body(g, False)
                body(GROUPS - 1, True)
                sp.dma_start(ident[:, :], ident_d).then_inc(id_loaded, 16)
                for t in range(XR):
                    load_x(sp, t)

            @block.scalar
            def _(act):
                act.wait_ge(u_loaded, 16)
                nc.scalar.activation(u_hi[:, :, :, :], u_raw[:, :, :, :], ACT.Copy).then_inc(u_high, 1)

                def high(g, n):
                    j, c = units[n]
                    at, w = CHUNKS[c]
                    act.wait_ge(gated, g * NU + n + 1)
                    nc.scalar.activation(a_hi[:, j, at:at + w], gated_f[:, n % 2, 0:w], ACT.Copy).then_inc(a_high, 1)

                def body(g, last):
                    act.wait_ge(v_loaded, g * 16 + 16)
                    reach(act, summed, g * NV)
                    nc.scalar.activation(v_hi[:, :, :], v_raw[:, :, :], ACT.Copy).then_inc(v_high, 1)
                    for n, (j, c) in enumerate(units):
                        w = CHUNKS[c][1]
                        act.wait_ge(hidden, g * NU + n + 1)
                        if n >= 2:
                            act.wait_ge(gated, g * NU + n - 1)
                        nc.scalar.activation(act_f[:, n % 2, 0:w], psum_u[:, c, 0:w], ACT.Gelu).then_inc(active, 1)
                        if n >= 1:
                            high(g, n - 1)
                    high(g, NU - 1)
                    if not last:
                        act.wait_ge(u_loaded, g * 16 + 32)
                        nc.scalar.activation(u_hi[:, :, :, :], u_raw[:, :, :, :], ACT.Copy).then_inc(u_high, 1)
                body(0, False)
                with act.Fori(1, GROUPS - 1) as g:
                    body(g, False)
                body(GROUPS - 1, True)

            @block.gpsimd
            def _(pool):
                def body(g):
                    pool.wait_ge(gate_loaded, g * 16 + 16)
                    for n, (j, c) in enumerate(units):
                        at, w = CHUNKS[c]
                        pool.wait_ge(active, g * NU + n + 1)
                        if n >= 2:
                            pool.wait_ge(a_low, g * NU + n - 1)
                        else:
                            reach(pool, a_low, g * NU)
                        nc.gpsimd.tensor_tensor(
                            gated_f[:, n % 2, 0:w].rearrange("p (b t) -> p b t", t=GB),
                            act_f[:, n % 2, 0:w].rearrange("p (b t) -> p b t", t=GB),
                            gate[:, at // GB:(at + w) // GB, j, :], ALU.mult).then_inc(gated, 1)
                body(0)
                with pool.Fori(1, GROUPS) as g:
                    body(g)

            @block.vector
            def _(dve):
                def split_u(g):
                    dve.wait_ge(u_high, g + 1)
                    nc.vector.tensor_tensor(u_lo[:, :, :, :], u_raw[:, :, :, :], u_hi[:, :, :, :].bitcast(F32),
                                            ALU.subtract).then_inc(u_low, 1)
                split_u(0)
                nc.vector.memset(y[:, :, :], 0.0).then_inc(cleared, 1)
                dve.wait_ge(cleared, 1)

                def body(g, last):
                    dve.wait_ge(v_high, g + 1)
                    nc.vector.tensor_tensor(v_lo[:, :, :], v_raw[:, :, :], v_hi[:, :, :].bitcast(F32),
                                            ALU.subtract).then_inc(v_low, 1)
                    for n, (j, c) in enumerate(units):
                        at, w = CHUNKS[c]
                        dve.wait_ge(a_high, g * NU + n + 1)
                        nc.vector.tensor_tensor(a_lo[:, j, at:at + w], gated_f[:, n % 2, 0:w],
                                                a_hi[:, j, at:at + w].bitcast(F32), ALU.subtract).then_inc(a_low, 1)
                    reach(dve, added, g * NV)
                    n = 0
                    for at, w in CHUNKS:
                        for d in range(KD):
                            dve.wait_ge(summed, g * NV + n + 1)
                            nc.vector.tensor_tensor(y[:, d, at:at + w], y[:, d, at:at + w],
                                                    psum_v[:, n % VB, 0:w], ALU.add).then_inc(added, 1)
                            n += 1
                            if n == KD and not last:
                                split_u(g + 1)
                body(0, False)
                with dve.Fori(1, GROUPS - 1) as g:
                    body(g, False)
                body(GROUPS - 1, True)

            @block.tensor
            def _(pe):
                def body(g):
                    pe.wait_ge(u_low, g + 1)
                    for n, (j, c) in enumerate(units):
                        at, w = CHUNKS[c]
                        if n >= 3:
                            pe.wait_ge(active, g * NU + n - 2)
                        else:
                            reach(pe, active, g * NU)
                        m = 0
                        for k in range(KD):
                            for a, b in ((u_hi, h_hi), (u_hi, h_lo), (u_lo, h_hi)):
                                last = nc.tensor.matmul(psum_u[:, c, 0:w], a[:, j, k, :], b[:, k, at:at + w],
                                                        start=(m == 0), stop=(m == 3 * KD - 1))
                                m += 1
                        last.then_inc(hidden, 1)
                    pe.wait_ge(v_low, g + 1)
                    n = 0
                    for c, (at, w) in enumerate(CHUNKS):
                        pe.wait_ge(a_low, g * NU + len(CHUNKS) * (JG - 1) + c + 1)
                        for d in range(KD):
                            if n >= VB:
                                pe.wait_ge(added, g * NV + n - VB + 1)
                            elif n == 0:
                                reach(pe, added, g * NV)
                            m = 0
                            for j in range(JG):
                                for a, b in ((v_hi, a_hi), (v_hi, a_lo), (v_lo, a_hi)):
                                    last = nc.tensor.matmul(psum_v[:, n % VB, 0:w], a[:, j, d * P:(d + 1) * P],
                                                            b[:, j, at:at + w], start=(m == 0), stop=(m == 3 * JG - 1))
                                    m += 1
                            last.then_inc(summed, 1)
                            n += 1
                body(0)
                with pe.Fori(1, GROUPS) as g:
                    body(g)

        with nc.Block() as block:
            turned, done, stored = sem("turned"), sem("done"), [sem(f"stored{i}") for i in range(XR)]

            @block.sync
            def _(sp):
                for t in range(NT):
                    sp.wait_ge(done, t + 1)
                    sp.dma_start(y_rows(t), x[0:rows_of(t), t % XR, :]).then_inc(stored[t % XR], 16)
                    if t >= 1 and t - 1 + XR < NT:
                        load_x(sp, t - 1 + XR)
                for i in range(XR):
                    sp.wait_ge(stored[i], 16 * ((NT - 1 - i) // XR + 1))

            @block.tensor
            def _(pe):
                pe.wait_ge(id_loaded, 16)
                for t in range(NT):
                    n = rows_of(t)
                    if t >= 2:
                        pe.wait_ge(done, t - 1)
                    for d in range(KD):
                        last = nc.tensor.transpose(psum_v[0:n, 2 * (t % 2) + d // 4, (d % 4) * P:(d % 4 + 1) * P],
                                                   y[:, d, t * P:t * P + n], ident[:, :])
                    last.then_inc(turned, 1)

            @block.vector
            def _(dve):
                for t in range(NT):
                    n = rows_of(t)
                    dve.wait_ge(x_loaded[t % XR], 16 * (t // XR + 1))
                    dve.wait_ge(turned, t + 1)
                    xt = x[0:n, t % XR, :].rearrange("p (a b) -> p a b", a=2)
                    nc.vector.tensor_tensor(xt, xt, psum_v[0:n, 2 * (t % 2):2 * (t % 2) + 2, :], ALU.add)\
                        .then_inc(done, 1)


C_IDENT, C_ONES, C_TRI, C_STRICT, C_LEVEL = (P * n for n in range(5))
C_EPS = C_LEVEL + (LEVELS + 1) * P
C_LNQ = C_EPS + 1
C_ONE = C_LNQ + 1
C_MIX = C_ONE + 1
C_IOTA = C_MIX
C_FLIP = C_IOTA + P
C_OUTSIDE = C_FLIP + P
C_STARTS = C_OUTSIDE + BAND
C_END = C_STARTS + TOPK
TOE = BAND + P - 1


def constants():
    i, j = np.arange(P)[:, None], np.arange(P)[None, :]
    out = np.zeros((P, C_END), np.float32)
    out[:, C_IDENT:C_IDENT + P] = i == j
    out[:, C_ONES:C_ONES + P] = 1
    out[:, C_TRI:C_TRI + P] = i <= j
    out[:, C_STRICT:C_STRICT + P] = i < j
    out[:, C_IOTA:C_IOTA + P] = j
    out[:, C_STARTS:C_STARTS + TOPK] = STARTS
    out[:, C_FLIP:C_FLIP + P] = i + j == P - 1
    for s in range(LEVELS):
        b = 1 << s
        out[:, C_LEVEL + s * P:C_LEVEL + (s + 1) * P] = (i // (2 * b) == j // (2 * b)) & (i // b % 2 == 1) & (j // b % 2 == 0)
    out[:, C_LEVEL + LEVELS * P:C_LEVEL + (LEVELS + 1) * P] = (i // 2 == j // 2) & (j % 2 == 1) & (i % 2 == 0)
    k = np.arange(BAND)[None, :]
    outside = ((i < CHUNK) & (k >= BAND - CHUNK)) | ((i >= CHUNK) & (k < CHUNK))
    out[:, C_OUTSIDE:C_OUTSIDE + BAND] = np.where(outside, np.float32(NEG), np.float32(0))
    out[:, C_EPS] = EPS
    out[:, C_LNQ] = np.log(DK ** -0.5)
    out[:, C_ONE] = 1
    return out


@contextmanager
def relative_bias_loads(nc, I, toeplitz):
    with ExitStack() as ctx:
        def sem(name):
            return ctx.enter_context(nc.semaphore(f"rb_{name}"))
        row = ctx.enter_context(nc.sbuf_tensor("rb_row", [H_AT, TOE], F32))
        skew = ctx.enter_context(nc.sbuf_tensor("rb_skew", [P, H_AT, BAND], F32))
        flip = ctx.enter_context(nc.sbuf_tensor("rb_flip", [P, P], F32))
        outside = ctx.enter_context(nc.sbuf_tensor("rb_outside", [P, BAND], F32))
        psum = ctx.enter_context(nc.psum_tensor("rb_psum", [P, 4, 512], F32))
        loaded, filled, written, flipped, masked = (sem("loaded"), sem("filled"), sem("written"), sem("flipped"),
                                                    sem("masked"))
        far = TOE - (N_REL - 1)
        parts = [(h, half) for h in range(H_AT) for half in range(2)]

        def loads(pool):
            pool.dma_start(row[:, far:TOE], I["rel_bias"][:, 0:N_REL - 1]).then_inc(loaded, 16)
            pool.dma_start(flip[:, :], I["consts"][:, C_FLIP:C_FLIP + P]).then_inc(loaded, 16)
            pool.dma_start(outside[:, :], I["consts"][:, C_OUTSIDE:C_OUTSIDE + BAND]).then_inc(loaded, 16)
            pool.wait_ge(loaded, 48)
            nc.gpsimd.tensor_copy(row[:, 0:far], row[:, far:far + 1].to_broadcast([H_AT, far])).then_inc(filled, 1)
            pool.wait_ge(filled, 1)
            pool.dma_start(toeplitz[:, :], row[:, :]).then_inc(written, 16)
            pool.wait_ge(written, 16)
            src = bass.AP(tensor=toeplitz.tensor, offset=0, ap=[[1, P], [TOE, H_AT], [1, BAND]])
            pool.dma_start(skew[:, :, :], src).then_inc(written, 16)
            pool.wait_ge(written, 32)

        def finish(bias):
            with nc.Block() as block:
                @block.vector
                def _(dve):
                    for n, (h, half) in enumerate(parts):
                        dve.wait_ge(flipped, n + 1)
                        cols = slice(half * BAND // 2, (half + 1) * BAND // 2)
                        nc.vector.tensor_tensor(bias[:, h, cols], psum[:, n % 4, 0:BAND // 2], outside[:, cols],
                                                ALU.add).then_inc(masked, 1)

                @block.tensor
                def _(pe):
                    for n, (h, half) in enumerate(parts):
                        if n >= 4:
                            pe.wait_ge(masked, n - 3)
                        nc.tensor.matmul(psum[:, n % 4, 0:BAND // 2], flip[:, :],
                                         skew[:, h, half * BAND // 2:(half + 1) * BAND // 2], start=True, stop=True)\
                            .then_inc(flipped, 1)
        yield loads, finish


def mix(nc, I, proj, x_tile, x2_tile, outs, bias):
    with ExitStack() as ctx:
        def sb(name, shape, dt=F32):
            return ctx.enter_context(nc.sbuf_tensor(f"mx_{name}", shape, dt))

        def sem(name):
            return ctx.enter_context(nc.semaphore(f"mx_{name}"))
        cs = sb("consts", [P, C_MIX])
        head_gain = sb("head_gain", [P, 2 * AT_W])
        conv_w = sb("conv_w", [P, CONV_BLOCKS, CONV_W])
        cat_gain = sb("cat_gain", [P, KD])
        dn_small = sb("dn_small", [P, 4, H_DN])
        consts = sem("consts")
        setup = sem("setup")
        with nc.Block() as block:
            @block.sync
            def _(sp):
                sp.dma_start(cs[:, :], I["consts"][:, 0:C_MIX]).then_inc(consts, 16)
                for half, name in enumerate(("q_norm", "k_norm")):
                    sp.dma_start(head_gain[:, half * AT_W:(half + 1) * AT_W].rearrange("p (h d) -> p h d", d=DH),
                                 I[name].unsqueeze(0).to_broadcast([P, H_AT, DH])).then_inc(consts, 16)
                sp.dma_start(dn_small[:, 0, :], I["a_log"].to_broadcast([P, H_DN])).then_inc(consts, 16)
                sp.dma_start(dn_small[:, 1, :], I["dt_bias"].to_broadcast([P, H_DN])).then_inc(consts, 16)
                sp.dma_start(conv_w[:, :, :], I["conv_w"]).then_inc(consts, 16)
                sp.dma_start(cat_gain[:, 0:H_DN], I["attn_norm"]).then_inc(consts, 16)
                for h in range(H_DN):
                    with nc.allow_non_contiguous_dma("128 numbers, one to a partition"):
                        sp.dma_start(cat_gain[:, H_DN + h:H_DN + h + 1], I["dn_norm"]).then_inc(consts, 16)

            @block.scalar
            def _(act):
                act.wait_ge(consts, 16 * 11)
                nc.scalar.activation(dn_small[:, 2, :], dn_small[:, 0, :], ACT.Exp).then_inc(setup, 1)

            @block.vector
            def _(dve):
                dve.wait_ge(setup, 1)
                nc.vector.tensor_scalar(dn_small[:, 3, :], dn_small[:, 2, :], -1.0, None, ALU.mult).then_inc(setup, 1)
                nc.vector.tensor_scalar(head_gain[:, 0:AT_W], head_gain[:, 0:AT_W], DH ** -0.5, None,
                                        ALU.mult).then_inc(setup, 1)
        mix_tiles(nc, I, proj, x_tile, x2_tile, outs, cs, bias, head_gain, conv_w, cat_gain, dn_small)


def interleave(*programs):
    heads = [[next(p), n, p] for n, p in enumerate(programs)]
    while heads:
        head = min(heads, key=lambda h: (h[0], h[1]))
        try:
            head[0] = next(head[2])
        except StopIteration:
            heads.remove(head)


KV_RING = BAND_TILES + 1
ON_DVE_PTC = 3
(EB, EB1, BETA, APRE, AABS, AMAX, AEXP, ASP, SPL, G, GCOL, GLG, EGC, EKD, BNEG, KSC, OSS, OLN, ORS) = range(19)


def mix_tiles(nc, I, proj, x_tile, x2_tile, outs, cs, bias, head_gain, conv_w, cat_gain, dn_small):
    ident = cs[:, C_IDENT:C_IDENT + P]
    ones = cs[:, C_ONES:C_ONES + P]
    tri = cs[:, C_TRI:C_TRI + P]
    eps = cs[:, C_EPS:C_EPS + 1]
    lnq = cs[:, C_LNQ:C_LNQ + 1]
    one = cs[:, C_ONE:C_ONE + 1]
    with ExitStack() as ctx:
        def sb(name, shape, dt=F32):
            return ctx.enter_context(nc.sbuf_tensor(f"mx_{name}", shape, dt))

        def sem(name):
            return ctx.enter_context(nc.semaphore(f"mx_{name}"))
        w_out = sb("w_out", [P, KD, D])
        w_loaded = sem("w_loaded")
        pj = sb("pj", [P, IN_W])
        cbuf = sb("cbuf", [P, CONV_BLOCKS, HALO + P])
        cy = sb("cy", [P, CONV_BLOCKS, P])
        csq = sb("csq", [P, 8, P])
        qkd = sb("qkd", [P, 8, P])
        wide = sb("wide", [P, 2 * AT_W])
        ssq, ssl, rsq = sb("ssq", [P, 16]), sb("ssl", [P, 16]), sb("rsq", [P, 16])
        grow, brow, dec = sb("grow", [P, 4, P]), sb("brow", [P, 4, P]), sb("dec", [P, 4, P])
        small = sb("small", [P, 19, H_DN])
        zs, qT = sb("zs", [P, 2, 4, P]), sb("qT", [P, 2, 4, P])
        kbn, kd, vb = sb("kbn", [P, 2, 4, P]), sb("kd", [P, 2, 4, P]), sb("vb", [P, 2, 4, P])
        qg, AT, QK = sb("qg", [P, 2, 4, P]), sb("AT", [P, 2, 4, P]), sb("QK", [P, 2, 4, P])
        eglast = sb("eglast", [P, 2, H_DN])
        kT = sb("kT", [P, 4, KV_RING, P])
        vh = sb("vh", [P, KV_RING, AT_W])
        T, Z, W = sb("T", [P, 4, P]), sb("Z", [P, 4, P]), sb("W", [P, 4, P])
        wT, vn, S = sb("wT", [P, 4, P]), sb("vn", [P, 4, P]), sb("S", [P, 4, P])
        oS, osq = sb("oS", [P, 4, P]), sb("osq", [P, 4, P])
        past_k = sb("past_k", [P, 2, AT_W])
        prob = sb("prob", [P, 2, BAND])
        probT = sb("probT", [P, BAND])
        top, ntop, sums, inv = (sb(n, [P, H_AT]) for n in ("top", "ntop", "sums", "inv"))
        ao = sb("ao", [P, AT_W])
        aosq = sb("aosq", [P, AT_W])
        stat = sb("stat", [P, 4])
        cat = sb("cat", [P, D])
        catT = sb("catT", [P, KD, P])
        xt = sb("xt", [P, D])
        SC, PTp, OB, X, Y, Zb = (ctx.enter_context(nc.psum_tensor(f"mx_bank{n}", [P, w * 512], F32))
                                 for n, w in enumerate((2, 2, 1, 1, 1, 1)))
        X3, Y3, Z3 = (b.ap().rearrange("p (h n) -> p h n", h=4) for b in (X, Y, Zb))

        lv = list(range(1, LEVELS))
        fp = Steps(sem("front_pe"), ["conv0", "conv1", "conv2", "gcol", "grow", "brow", "qT", "kT", "normq", "normk",
                                     "k", "v", "kk", "qk"])
        fa = Steps(sem("front_act"), ["expb", "absexp", "lnsp", "conv0", "conv1", "conv2", "grow", "brow", "egrow",
                                      "sq", "silu", "siluz", "sqln", "rsq", "csq", "qT", "expcol", "dec", "kT",
                                      "lnq", "lnk", "rs"])
        fd = Steps(sem("front_dve"), ["halo", "eb1", "beta", "apre", "aabs", "amax", "sp", "g", "gz"]
                   + [x for n in range(3 * CONV_W) for x in
                      (["gcol"] if n == 5 else []) + [f"tap{n // CONV_W}{n % CONV_W}"]]
                   + ["ssq", "qkn0", "qkn", "dif", "glg", "egl", "decT", "m1", "bneg", "kscale", "strict", "qkd",
                      "qg", "kbn", "kd", "vb", "AT", "QK"])
        cp = Steps(sem("core_pe"), ["A"] + [f"{a}{s}" for s in lv for a in ("w", "t", "z")] + ["wT", "vn", "o", "ds"])
        ca = Steps(sem("core_act"), ["wT", "vn", "o", "osq", "oln", "ors"])
        cd = Steps(sem("core_dve"), ["T0", "T", "Z0", "Z"] + [f"{a}{s}" for s in lv for a in ("W", "T", "Z")]
                   + ["oss", "S", "oz", "cat1"])
        ap_ = Steps(sem("attend_pe"), [x for h in range(H_AT + 2) for x in
                                       ([f"pv{h - 2}"] if h >= 2 else []) + ([f"sc{h}"] if h < H_AT else [])
                                       + ([f"pt{h - 1}"] if 1 <= h <= H_AT else [])])
        aa = Steps(sem("attend_act"), [x for h in range(H_AT + 1) for x in
                                       ([f"ptc{h - 1}"] if h and h - 1 != ON_DVE_PTC else []) + ([f"exp{h}"] if h < H_AT else [])]
                   + ["aosq", "aoln", "aors", "cat0"])
        ad = Steps(sem("attend_dve"), [f"{a}{h}" for h in range(H_AT) for a in ("sm", "nt")]
                   + ["inv", "ao"])
        ad.names.insert(ad.names.index(f"sm{ON_DVE_PTC + 1}"), f"ptc{ON_DVE_PTC}")
        op, od = Steps(sem("out_pe"), ["catT", "out0", "out1"]), Steps(sem("out_dve"), ["catT", "x2a", "x2b"])
        pj_loaded, vh_loaded = sem("pj_loaded"), sem("vh_loaded")
        x_loaded, x2_stored, kept, k_kept = sem("x_loaded"), sem("x2_stored"), sem("kept"), sem("k_kept")
        pastk_loaded, pastv_loaded = [sem("pastk_loaded0"), sem("pastk_loaded1")], sem("pastv_loaded")
        halo_loaded, state_loaded = sem("halo_loaded"), sem("state_loaded")
        past_turned, past_copied, init = sem("past_turned"), sem("past_copied"), sem("init")
        block = ctx.enter_context(nc.Block())

        def band(t):
            seen = min(t, PAST_TILES) if t < PT else PAST_TILES
            slots = [(t - seen + n) % KV_RING for n in range(seen + 1)]
            return slots, (BAND_TILES - len(slots)) * P

        def core_tick(s, part):
            early = {1: (1.7, 2.0, 4.2, 4.35), 2: (7.2, 8.4, 10, 11)}
            return early[s][part] if s in early else 4 * s + part

        def on(eng, steps, t, name):
            if t >= 0:
                eng.wait_ge(steps.sem, steps.at(t, name))

        def run_tiles(front, core, attend, finish):
            interleave(front(0))
            for t in range(NT):
                interleave(core(t), attend(t), *([finish(t - 1)] if t else []), *([front(t + 1)] if t + 1 < NT else []))
            interleave(finish(NT - 1))

        def nothing(t):
            yield 0

        @block.sync
        def _(sp):
            def front_loads(t):
                if t >= 1:
                    on(sp, fp, t - 1, "conv2")
                    on(sp, fa, t - 1, "siluz")
                    on(sp, fd, t - 1, "qkn0")
                sp.dma_start(pj[:, :], proj[t * P:(t + 1) * P, :]).then_inc(pj_loaded, 16)
                on(sp, ap_, t - 2, f"pv{H_AT - 1}")
                sp.dma_start(vh[:, t % KV_RING, :], proj[t * P:(t + 1) * P, C_AV:C_AV + AT_W]).then_inc(vh_loaded, 16)
                if t == PT:
                    on(sp, fd, t - 1, "tap23")
                    with nc.allow_non_contiguous_dma("three rows before the sample's"):
                        sp.dma_start(cbuf[:, :, 0:HALO], I["conv_state"]).then_inc(halo_loaded, 16)

            sp.wait_ge(init, 1)
            front_loads(0)
            sp.dma_start(w_out[:, :, :], I["w_out"].rearrange("(k p) n -> p k n", p=P)).then_inc(w_loaded, 16)
            first = SEQ - WINDOW
            sp.dma_start(outs["p_v"], proj[first:SEQ, C_AV:C_AV + AT_W]).then_inc(kept, 16)
            sp.dma_start(outs["s_v"], proj[SEQ:TOK, C_AV:C_AV + AT_W]).then_inc(kept, 16)
            sp.dma_start(outs["p_conv"], proj[SEQ - HALO:SEQ, C_DN:C_DN + CONV_CH]).then_inc(kept, 16)
            sp.dma_start(outs["s_conv"], proj[TOK - HALO:TOK, C_DN:C_DN + CONV_CH]).then_inc(kept, 16)

            def keep_keys(t):
                if t >= PT - PAST_TILES:
                    on(sp, fd, t, "qkn")
                    dst = (outs["p_k"][(t - PT + PAST_TILES) * P:(t - PT + PAST_TILES + 1) * P, :] if t < PT
                           else outs["s_k"])
                    sp.dma_start(dst, wide[0:rows_of(t), AT_W:2 * AT_W]).then_inc(k_kept, 16)
            for t in range(NT):
                n = rows_of(t)
                if t == PT:
                    on(sp, ap_, t - 1, f"pv{H_AT - 1}")
                    for m in range(PAST_TILES):
                        slot = (t - PAST_TILES + m) % KV_RING
                        sp.dma_start(vh[:, slot, :], I["cache_v"][m * P:(m + 1) * P, :]).then_inc(pastv_loaded, 16)
                        if m >= 2:
                            sp.wait_ge(past_turned, m - 1)
                        sp.dma_start(past_k[:, m % 2, :], I["cache_k"][m * P:(m + 1) * P, :])\
                            .then_inc(pastk_loaded[m % 2], 16)
                if t + 1 < NT:
                    front_loads(t + 1)
                if t >= 1:
                    on(sp, od, t - 1, "x2b")
                    sp.dma_start(x2_tile(t - 1), xt[0:rows_of(t - 1), :]).then_inc(x2_stored, 16)
                    sp.wait_ge(x2_stored, 16 * t)
                sp.dma_start(xt[0:n, :], x_tile(t)).then_inc(x_loaded, 16)
                if t + 1 < NT:
                    keep_keys(t + 1)
                if t == PT - 1:
                    on(sp, cd, t, "S")
                    sp.dma_start(outs["p_state"].rearrange("h k v -> k h v"), S[:, :, :]).then_inc(kept, 16)
                    sp.wait_ge(kept, 16 * 5)
                    sp.dma_start(S[:, :, :], I["state"].rearrange("h k v -> k h v")).then_inc(state_loaded, 16)
            on(sp, od, NT - 1, "x2b")
            sp.dma_start(x2_tile(NT - 1), xt[0:DEC, :]).then_inc(x2_stored, 16)
            on(sp, cd, NT - 1, "S")
            sp.dma_start(outs["s_state"].rearrange("h k v -> k h v"), S[:, :, :]).then_inc(kept, 16)
            sp.wait_ge(kept, 16 * 6)
            sp.wait_ge(k_kept, 16 * (NT - PT + PAST_TILES))
            sp.wait_ge(x2_stored, 16 * NT)

        @block.scalar
        def _(act):
            def step(steps, name, out, in_, func, **kw):
                nc.scalar.activation(out, in_, func, **kw).then_inc(steps.sem, steps.one(name))

            def front(t):
                par = t % 2
                yield 1.1
                act.wait_ge(pj_loaded, 16 * (t + 1))
                on(act, fd, t - 1, "kscale")
                step(fa, "expb", small[:, EB, :], pj[:, C_B:C_B + H_DN], ACT.Exp, scale=-1.0)
                on(act, fd, t, "aabs")
                step(fa, "absexp", small[:, AEXP, :], small[:, AABS, :], ACT.Exp, scale=-1.0)
                on(act, fa, t, "absexp")
                step(fa, "lnsp", small[:, SPL, :], small[:, AEXP, :], ACT.Ln, bias=one)
                on(act, fd, t, "halo")
                for r in range(3):
                    yield 2 + 2 * r
                    on(act, fp, t, f"conv{r}")
                    step(fa, f"conv{r}", cbuf[:, 4 * r:4 * r + 4, HALO:], Z3, ACT.Copy)
                yield 11
                on(act, fp, t, "grow")
                step(fa, "grow", grow[:, :, :], Z3, ACT.Copy)
                yield 13
                on(act, fp, t, "brow")
                step(fa, "brow", brow[:, :, :], Z3, ACT.Copy)
                on(act, fa, t, "grow")
                on(act, cp, t - 2, "o")
                on(act, cd, t - 2, "S")
                step(fa, "egrow", qg[:, par, :, :], grow[:, :, :], ACT.Exp)
                yield 15
                if t > PT - PAST_TILES:
                    act.wait_ge(k_kept, 16 * (t - PT + PAST_TILES))
                on(act, fp, t - 1, "kT")
                step(fa, "sq", wide[:, :], pj[:, 0:2 * AT_W], ACT.Square)
                yield 15.9
                on(act, fd, t, "tap23")
                nc.scalar.preload_act_table_set("silu_and_others")
                step(fa, "silu", cy[:, :, :], cy[:, :, :], ACT.Silu)
                on(act, cd, t - 2, "cat1")
                step(fa, "siluz", zs[:, par, :, :].rearrange("p h n -> p (h n)"), pj[:, C_Z:C_Z + DN_W], ACT.Silu)
                nc.scalar.preload_act_table_set("natural_log_exp_and_others")
                yield 18.5
                on(act, fd, t, "ssq")
                step(fa, "sqln", ssl[:, :], ssq[:, :], ACT.Ln, scale=1.0 / DH, bias=eps)
                on(act, fa, t, "sqln")
                step(fa, "rsq", rsq[:, :], ssl[:, :], ACT.Exp, scale=-0.5)
                yield 19.2
                on(act, fa, t, "silu")
                step(fa, "csq", csq[:, :, :], cy[:, 0:8, :], ACT.Square)
                yield 21.7
                on(act, fp, t, "qT")
                on(act, ap_, t - 2, f"sc{H_AT - 1}")
                step(fa, "qT", qT[:, par, :, :], Z3, ACT.Copy)
                yield 22
                on(act, fd, t, "glg")
                step(fa, "expcol", small[:, EGC:EKD + 1, :], small[:, GCOL:GLG + 1, :], ACT.Exp)
                step(fa, "dec", dec[:, :, :], dec[:, :, :], ACT.Exp)
                yield 23.3
                on(act, fp, t, "kT")
                step(fa, "kT", kT[:, :, t % KV_RING, :], Z3, ACT.Copy)
                for n, name in enumerate("qk"):
                    yield 25.3 + 2 * n
                    on(act, fp, t, f"norm{name}")
                    step(fa, f"ln{name}", csq[:, 4 * n:4 * n + 4, :], Z3, ACT.Ln, bias=eps)
                on(act, fa, t, "lnk")
                nc.scalar.activation(csq[:, 0:4, :], csq[:, 0:4, :], ACT.Exp, scale=-0.5, bias=lnq)
                step(fa, "rs", csq[:, 4:8, :], csq[:, 4:8, :], ACT.Exp, scale=-0.5)

            def core(t):
                yield 29
                on(act, cp, t, "wT")
                step(ca, "wT", wT[:, :, :], X3, ACT.Copy)
                yield 31
                on(act, cp, t, "vn")
                step(ca, "vn", vn[:, :, :], Y3, ACT.Copy)
                yield 33
                on(act, cp, t, "o")
                step(ca, "o", oS[:, :, :], X3, ACT.Copy)
                on(act, ca, t, "o")
                on(act, cd, t - 1, "cat1")
                step(ca, "osq", osq[:, :, :], oS[:, :, :], ACT.Square)
                yield 35
                on(act, cd, t, "oss")
                step(ca, "oln", small[:, OLN, :], small[:, OSS, :], ACT.Ln, scale=1.0 / DK, bias=eps)
                on(act, ca, t, "oln")
                step(ca, "ors", small[:, ORS, :], small[:, OLN, :], ACT.Exp, scale=-0.5)

            def attend(t):
                slots, at = band(t)
                nk = len(slots) * P
                yield 0
                if t == PT:
                    for m in range(PAST_TILES):
                        act.wait_ge(past_turned, m + 1)
                        nc.scalar.activation(kT[:, :, (t - PAST_TILES + m) % KV_RING, :],
                                             SC[:, 512 * (m % 2):512 * (m % 2) + 512].rearrange("p (a n) -> p a n", a=4),
                                             ACT.Copy).then_inc(past_copied, 1)
                for h in range(H_AT + 1):
                    if h >= 1 and h - 1 != ON_DVE_PTC:
                        yield 4 * h + 1.8
                        on(act, ap_, t, f"pt{h - 1}")
                        if h >= 2:
                            on(act, ap_, t, f"pv{h - 2}")
                        step(aa, f"ptc{h - 1}", probT[:, 0:nk], PTp[:, 0:nk], ACT.Copy)
                    if h < H_AT:
                        yield 4 * h + 2.3
                        on(act, ad, t, f"nt{h}")
                        step(aa, f"exp{h}", prob[:, h % 2, 0:nk], prob[:, h % 2, 0:nk], ACT.Exp, bias=ntop[:, h:h + 1],
                             accum_out=sums[:, h:h + 1])
                yield 36.1
                on(act, ad, t, "ao")
                step(aa, "aosq", aosq[:, :], ao[:, :], ACT.Square, accum_out=stat[:, 0:1])
                on(act, aa, t, "aosq")
                step(aa, "aoln", stat[:, 1:2], stat[:, 0:1], ACT.Ln, scale=1.0 / AT_W, bias=eps)
                on(act, aa, t, "aoln")
                step(aa, "aors", stat[:, 2:3], stat[:, 1:2], ACT.Exp, scale=-0.5)
                on(act, aa, t, "aors")
                on(act, op, t - 1, "catT")
                step(aa, "cat0", cat[:, 0:AT_W], ao[:, :], ACT.Copy, scale=stat[:, 2:3])
            nc.scalar.preload_act_table_set("natural_log_exp_and_others")
            run_tiles(front, core, attend, nothing)

        @block.vector
        def _(dve):
            nc.vector.memset(S[:, :, :], 0.0)
            nc.vector.memset(xt[:, :], 0.0)
            nc.vector.memset(cbuf[:, :, 0:HALO], 0.0).then_inc(init, 1)
            dve.wait_ge(init, 1)
            tt_, ts_ = nc.vector.tensor_tensor, nc.vector.tensor_scalar

            def step(steps, name, ins):
                ins.then_inc(steps.sem, steps.one(name))

            def then(steps, t, name, ins):
                step(steps, name, ins)
                on(dve, steps, t, name)

            def level(s):
                return cs[:, C_LEVEL + s * P:C_LEVEL + (s + 1) * P].unsqueeze(1).to_broadcast([P, 4, P])
            ident4 = ident.unsqueeze(1).to_broadcast([P, 4, P])

            def front(t):
                par = t % 2
                yield 0
                if 0 < t < PT:
                    on(dve, fd, t - 1, "tap23")
                    step(fd, "halo", nc.vector.tensor_copy(cbuf[:, :, 0:HALO], cbuf[:, :, P:P + HALO]))
                else:
                    if t == PT:
                        dve.wait_ge(halo_loaded, 16)
                    step(fd, "halo", nc.vector.tensor_copy(stat[:, 3:4], one))
                yield 1.2
                on(dve, fa, t, "expb")
                then(fd, t, "eb1", ts_(small[:, EB1, :], small[:, EB, :], 1.0, None, ALU.add))
                on(dve, fp, t - 1, "brow")
                step(fd, "beta", nc.vector.reciprocal(small[:, BETA, :], small[:, EB1, :]))
                then(fd, t, "apre", tt_(small[:, APRE, :], pj[:, C_A:C_A + H_DN], dn_small[:, 1, :], ALU.add))
                step(fd, "aabs", nc.vector.scalar_tensor_tensor(small[:, AABS, :], small[:, APRE, :], -1.0,
                                                                small[:, APRE, :], ALU.mult, ALU.max))
                then(fd, t, "amax", ts_(small[:, AMAX, :], small[:, APRE, :], 0.0, None, ALU.max))
                on(dve, fa, t, "lnsp")
                then(fd, t, "sp", tt_(small[:, ASP, :], small[:, AMAX, :], small[:, SPL, :], ALU.add))
                then(fd, t, "g", tt_(small[:, G, :], small[:, ASP, :], dn_small[:, 3, :], ALU.mult))
                if t == PT:
                    nc.vector.memset(small[DEC:P, BETA, :], 0.0)
                    step(fd, "gz", nc.vector.memset(small[DEC:P, G, :], 0.0))
                else:
                    step(fd, "gz", nc.vector.tensor_copy(stat[:, 3:4], one))

                def taps(r, i):
                    if i == 0:
                        on(dve, fa, t, f"conv{r}")
                        on(dve, fp, t - 1, "v")
                    else:
                        on(dve, fd, t, f"tap{r}{i - 1}")
                    for c in range(4 * r, 4 * r + 4):
                        src, w = cbuf[:, c, i:i + P], conv_w[:, c, i:i + 1]
                        if i == 0:
                            last = ts_(cy[:, c, :], src, w, None, ALU.mult)
                        else:
                            last = nc.vector.scalar_tensor_tensor(cy[:, c, :], src, w, cy[:, c, :], ALU.mult, ALU.add)
                    step(fd, f"tap{r}{i}", last)
                for n, tick in enumerate((2.5, 3.5, 5.5, 6.5, 7.5, 9.5, 10.5, 11.5, 13.5, 14.5, 15.5, 15.7)):
                    if n == 5:
                        yield 9.2
                        on(dve, fp, t, "gcol")
                        step(fd, "gcol", nc.vector.tensor_copy(small[:, GCOL, :], Zb[:, 0:H_DN]))
                    yield tick
                    taps(n // CONV_W, n % CONV_W)
                yield 18.1
                on(dve, fa, t, "sq")
                step(fd, "ssq", nc.vector.tensor_reduce(ssq[:, :], wide[:, :].rearrange("p (h d) -> p h d", d=DH),
                                                        AX.X, ALU.add))
                yield 19.1
                on(dve, fa, t, "rsq")
                step(fd, "qkn0", tt_(wide[:, :].rearrange("p (h d) -> p h d", d=DH),
                                     pj[:, 0:2 * AT_W].rearrange("p (h d) -> p h d", d=DH),
                                     rsq[:, :].unsqueeze(2).to_broadcast([P, 16, DH]), ALU.mult))
                yield 21.02
                on(dve, fd, t, "qkn0")
                step(fd, "qkn", tt_(wide[:, :], wide[:, :], head_gain[:, :], ALU.mult))
                yield 21.5
                on(dve, fa, t, "grow")
                for h in range(H_DN):
                    last = ts_(dec[:, h, :], grow[:, h, :], small[:, GCOL, h:h + 1], 0.0, ALU.subtract, ALU.min)
                step(fd, "dif", last)
                step(fd, "glg", tt_(small[:, GLG, :], grow[:, :, P - 1], small[:, GCOL, :], ALU.subtract))
                on(dve, fa, t, "egrow")
                on(dve, cd, t - 2, "S")
                step(fd, "egl", nc.vector.tensor_copy(eglast[:, par, :], qg[:, par, :, P - 1]))
                yield 23.5
                on(dve, fa, t, "dec")
                then(fd, t, "decT", tt_(dec[:, :, :], dec[:, :, :], tri.unsqueeze(1).to_broadcast([P, 4, P]), ALU.mult))
                on(dve, cp, t - 2, f"w{lv[-1]}")
                then(fd, t, "m1", tt_(AT[:, par, :, :], dec[:, :, :], brow[:, :, :], ALU.mult))
                yield 25.5
                then(fd, t, "bneg", ts_(small[:, BNEG, :], small[:, BETA, :], -1.0, None, ALU.mult))
                step(fd, "kscale", tt_(small[:, KSC, :], small[:, BNEG, :], small[:, EGC, :], ALU.mult))
                step(fd, "strict", tt_(AT[:, par, :, :], AT[:, par, :, :],
                                       cs[:, C_STRICT:C_STRICT + P].unsqueeze(1).to_broadcast([P, 4, P]), ALU.mult))
                yield 28.6
                on(dve, fa, t, "rs")
                then(fd, t, "qkd", tt_(qkd[:, :, :], cy[:, 0:8, :], csq[:, :, :], ALU.mult))
                step(fd, "qg", tt_(qg[:, par, :, :], qkd[:, 0:4, :], qg[:, par, :, :], ALU.mult))
                yield 31.5
                on(dve, fp, t, "k")
                for h in range(H_DN):
                    last = ts_(kbn[:, par, h, :], Z3[:, h, :], small[:, KSC, h:h + 1], None, ALU.mult)
                step(fd, "kbn", last)
                for h in range(H_DN):
                    last = ts_(kd[:, par, h, :], Z3[:, h, :], small[:, EKD, h:h + 1], None, ALU.mult)
                step(fd, "kd", last)
                yield 33.2
                on(dve, fp, t, "v")
                for h in range(H_DN):
                    last = ts_(vb[:, par, h, :], Z3[:, h, :], small[:, BETA, h:h + 1], None, ALU.mult)
                step(fd, "vb", last)
                yield 35.1
                on(dve, fp, t, "kk")
                on(dve, fd, t, "strict")
                step(fd, "AT", tt_(AT[:, par, :, :], Z3, AT[:, par, :, :], ALU.mult))
                yield 37.2
                on(dve, fp, t, "qk")
                step(fd, "QK", tt_(QK[:, par, :, :], Z3, dec[:, :, :], ALU.mult))

            def core(t):
                par = t % 2
                yield 1
                on(dve, cp, t, "A")
                then(cd, t, "T0", tt_(W[:, :, :], X3, level(0), ALU.mult))
                then(cd, t, "T", tt_(T[:, :, :], ident4, W[:, :, :], ALU.subtract))
                then(cd, t, "Z0", tt_(W[:, :, :], AT[:, par, :, :], level(LEVELS), ALU.mult))
                step(cd, "Z", tt_(Z[:, :, :], ident4, W[:, :, :], ALU.subtract))
                for s in lv:
                    yield core_tick(s, 1)
                    on(dve, cp, t, f"w{s}")
                    step(cd, f"W{s}", tt_(W[:, :, :], X3, level(s), ALU.mult))
                    yield core_tick(s, 3)
                    on(dve, cp, t, f"t{s}")
                    on(dve, cp, t, f"z{s}")
                    step(cd, f"T{s}", tt_(T[:, :, :], T[:, :, :], Y3, ALU.subtract))
                    step(cd, f"Z{s}", tt_(Z[:, :, :], Z[:, :, :], X3, ALU.subtract))
                yield 34
                on(dve, ca, t, "osq")
                step(cd, "oss", nc.vector.tensor_reduce(small[:, OSS, :], osq[:, :, :], AX.X, ALU.add))
                yield 35.3
                on(dve, cp, t, "ds")
                for h in range(H_DN):
                    last = nc.vector.scalar_tensor_tensor(S[:, h, :], S[:, h, :], eglast[:, par, h:h + 1],
                                                          Y3[:, h, :], ALU.mult, ALU.add)
                step(cd, "S", last)
                yield 36
                on(dve, ca, t, "ors")
                then(cd, t, "oz", tt_(osq[:, :, :], oS[:, :, :], small[:, ORS, :].unsqueeze(2)
                                      .to_broadcast([P, 4, P]), ALU.mult))
                on(dve, op, t - 1, "catT")
                step(cd, "cat1", tt_(cat[:, AT_W:D].rearrange("p (h n) -> p h n", h=4), osq[:, :, :],
                                     zs[:, par, :, :], ALU.mult))

            def attend(t):
                slots, at = band(t)
                nk = len(slots) * P
                for h in range(H_AT):
                    if h - 1 == ON_DVE_PTC:
                        yield 4 * h + 1.8
                        on(dve, ap_, t, f"pt{h - 1}")
                        on(dve, ap_, t, f"pv{h - 2}")
                        step(ad, f"ptc{h - 1}", nc.vector.tensor_copy(probT[:, 0:nk], PTp[:, 0:nk]))
                    yield 4 * h + 2
                    on(dve, ap_, t, f"sc{h}")
                    if h >= 2:
                        on(dve, ap_, t, f"pt{h - 2}")
                    then(ad, t, f"sm{h}", nc.vector.tensor_tensor_reduce(
                        prob[:, h % 2, 0:nk], SC[:, 0:nk], bias[:, h, at:at + nk], 1.0, NEG, ALU.add, ALU.max,
                        top[:, h:h + 1]))
                    step(ad, f"nt{h}", ts_(ntop[:, h:h + 1], top[:, h:h + 1], -1.0, None, ALU.mult))
                yield 35.9
                on(dve, aa, t, f"exp{H_AT - 1}")
                then(ad, t, "inv", nc.vector.reciprocal(inv[:, :], sums[:, :]))
                on(dve, ap_, t, f"pv{H_AT - 1}")
                step(ad, "ao", tt_(ao[:, :].rearrange("p (h d) -> p h d", d=DH),
                                   OB.ap().rearrange("p (h d) -> p h d", d=DH),
                                   inv[:, :].unsqueeze(2).to_broadcast([P, H_AT, DH]), ALU.mult))

            def finish(t):
                yield 1.15
                on(dve, op, t, "catT")
                on(dve, op, t - 1, "out1")
                step(od, "catT", tt_(catT[:, :, :], PTp.ap().rearrange("p (k n) -> p k n", k=KD),
                                     cat_gain[:, :].unsqueeze(2).to_broadcast([P, KD, P]), ALU.mult))
                for half in range(2):
                    yield 3.4 + 3.5 * half
                    on(dve, op, t, f"out{half}")
                    dve.wait_ge(x_loaded, 16 * (t + 1))
                    cols = slice(half * 512, (half + 1) * 512)
                    step(od, f"x2{'ab'[half]}", tt_(xt[:, cols], xt[:, cols], OB.ap(), ALU.add))
            run_tiles(front, core, attend, finish)

        @block.tensor
        def _(pe):
            mm, tr = nc.tensor.matmul, nc.tensor.transpose

            def done(steps, name, ins):
                ins.then_inc(steps.sem, steps.one(name))

            def heads(out, lhs, rhs):
                for h in range(H_DN):
                    last = mm(out[:, h, :], lhs[:, h, :], rhs[:, h, :], start=True, stop=True)
                return last

            def front(t):
                yield 1
                pe.wait_ge(pj_loaded, 16 * (t + 1))
                on(pe, fd, t - 1, "QK")
                for r in range(3):
                    if r:
                        yield 1 + 2 * r
                        on(pe, fa, t, f"conv{r - 1}")
                    for c in range(4):
                        col = C_DN + (4 * r + c) * P
                        last = tr(Z3[:, c, :], pj[:, col:col + P], ident)
                    done(fp, f"conv{r}", last)
                yield 8
                on(pe, fa, t, "conv2")
                on(pe, fd, t, "gz")
                on(pe, fd, t, "beta")
                done(fp, "gcol", mm(Zb[:, 0:H_DN], tri, small[:, G, :], start=True, stop=True))
                yield 10
                on(pe, fd, t, "gcol")
                for h in range(H_DN):
                    last = mm(Z3[:, h, :], small[:, G, h:h + 1].to_broadcast([P, P]), tri, start=True, stop=True)
                done(fp, "grow", last)
                yield 12
                on(pe, fa, t, "grow")
                for h in range(H_DN):
                    last = mm(Z3[:, h, :], small[:, BETA, h:h + 1].to_broadcast([P, P]), ident, start=True, stop=True)
                done(fp, "brow", last)
                yield 21.6
                on(pe, fd, t, "qkn")
                on(pe, fa, t, "brow")
                for c in range(4):
                    last = tr(Z3[:, c, :], wide[:, c * P:(c + 1) * P], ident)
                done(fp, "qT", last)
                yield 22.3
                on(pe, fa, t, "qT")
                for c in range(4):
                    last = tr(Z3[:, c, :], wide[:, AT_W + c * P:AT_W + (c + 1) * P], ident)
                done(fp, "kT", last)
                for n, name in enumerate("qk"):
                    yield 24.3 + 2 * n
                    on(pe, fa, t, "csq")
                    on(pe, fa, t, "lnq" if n else "kT")
                    done(fp, f"norm{name}", mm(Zb[:, :], ones, csq[:, 4 * n:4 * n + 4, :]
                                               .rearrange("p h n -> p (h n)"), start=True, stop=True))
                yield 30.2
                on(pe, fd, t, "qkd")
                for h in range(H_DN):
                    last = tr(Z3[:, h, :], qkd[:, 4 + h, :], ident)
                done(fp, "k", last)
                yield 32.3
                on(pe, fd, t, "kd")
                for h in range(H_DN):
                    last = tr(Z3[:, h, :], cy[:, 8 + h, :], ident)
                done(fp, "v", last)
                yield 34.3
                on(pe, fd, t, "vb")
                done(fp, "kk", heads(Z3, qkd[:, 4:8, :], qkd[:, 4:8, :]))
                yield 36.2
                on(pe, fd, t, "AT")
                done(fp, "qk", heads(Z3, qkd[:, 4:8, :], qkd[:, 0:4, :]))

            def core(t):
                par = t % 2
                yield 0
                on(pe, fd, t, "AT")
                on(pe, ca, t - 1, "o")
                for h in range(H_DN):
                    last = tr(X3[:, h, :], AT[:, par, h, :], ident)
                done(cp, "A", last)
                for s in lv:
                    yield core_tick(s, 0)
                    on(pe, cd, t, "Z" if s == 1 else f"Z{s - 1}")
                    if s == 1:
                        on(pe, cd, t - 1, "S")
                    done(cp, f"w{s}", heads(X3, AT[:, par, :, :], T))
                    yield core_tick(s, 2)
                    on(pe, cd, t, f"W{s}")
                    done(cp, f"t{s}", heads(Y3, Z, W))
                    done(cp, f"z{s}", heads(X3, W, Z))
                yield 28
                on(pe, cd, t, f"Z{lv[-1]}")
                on(pe, fd, t, "vb")
                done(cp, "wT", heads(X3, kbn[:, par, :, :], Z))
                yield 30
                on(pe, ca, t, "wT")
                on(pe, cd, t - 1, "S")
                if t == PT:
                    pe.wait_ge(state_loaded, 16)
                for h in range(H_DN):
                    mm(Y3[:, h, :], Z[:, h, :], vb[:, par, h, :], start=True, stop=False)
                    last = mm(Y3[:, h, :], wT[:, h, :], S[:, h, :], start=False, stop=True)
                done(cp, "vn", last)
                yield 32
                on(pe, fd, t, "QK")
                on(pe, ca, t, "vn")
                for h in range(H_DN):
                    mm(X3[:, h, :], qg[:, par, h, :], S[:, h, :], start=True, stop=False)
                    last = mm(X3[:, h, :], QK[:, par, h, :], vn[:, h, :], start=False, stop=True)
                done(cp, "o", last)
                done(cp, "ds", heads(Y3, kd[:, par, :, :], vn))

            def attend(t):
                slots, at = band(t)
                yield 0.5
                if t == PT:
                    on(pe, ad, t - 1, f"sm{H_AT - 1}")
                    for m in range(PAST_TILES):
                        pe.wait_ge(pastk_loaded[m % 2], 16 * (m // 2 + 1))
                        if m >= 2:
                            pe.wait_ge(past_copied, m - 1)
                        for c in range(4):
                            last = tr(SC[:, (m % 2) * 512 + c * P:(m % 2) * 512 + (c + 1) * P],
                                      past_k[:, m % 2, c * P:(c + 1) * P], ident)
                        last.then_inc(past_turned, 1)
                    pe.wait_ge(past_copied, PAST_TILES)
                    pe.wait_ge(pastv_loaded, 16 * PAST_TILES)
                on(pe, fa, t, "kT")
                for h in range(H_AT + 2):
                    if h >= 2:
                        yield 4 * h - 0.5
                        if h == 2:
                            pe.wait_ge(vh_loaded, 16 * (t + 1))
                            on(pe, od, t - 1, "x2b")
                        on(pe, ad if h - 2 == ON_DVE_PTC else aa, t, f"ptc{h - 2}")
                        for n, s in enumerate(slots):
                            last = mm(OB[:, (h - 2) * DH:(h - 1) * DH], probT[:, n * P:(n + 1) * P],
                                      vh[:, s, (h - 2) * DH:(h - 1) * DH], start=(n == 0), stop=(n == len(slots) - 1))
                        done(ap_, f"pv{h - 2}", last)
                    if h < H_AT:
                        yield 4 * h + 1
                        on(pe, ad, t if h else t - 1, f"sm{(h - 1) % H_AT}")
                        r = slice(DH * (h % 2), DH * (h % 2) + DH)
                        for n, s in enumerate(slots):
                            last = mm(SC[:, n * P:(n + 1) * P], qT[r, t % 2, h // 2, :], kT[r, h // 2, s, :],
                                      start=True, stop=True)
                        done(ap_, f"sc{h}", last)
                    if 1 <= h <= H_AT:
                        yield 4 * h + 1.5
                        on(pe, aa, t, f"exp{h - 1}")
                        if h >= 2:
                            on(pe, ad if h - 2 == ON_DVE_PTC else aa, t, f"ptc{h - 2}")
                        else:
                            on(pe, od, t - 1, "catT")
                        for n in range(len(slots)):
                            last = tr(PTp[:, n * P:(n + 1) * P], prob[:, (h - 1) % 2, n * P:(n + 1) * P], ident)
                        done(ap_, f"pt{h - 1}", last)

            def finish(t):
                yield 1.12
                on(pe, aa, t, "cat0")
                on(pe, cd, t, "cat1")
                for k in range(KD):
                    last = tr(PTp[:, k * P:(k + 1) * P], cat[:, k * P:(k + 1) * P], ident)
                done(op, "catT", last)
                if t == 0:
                    pe.wait_ge(w_loaded, 16)
                for half in range(2):
                    for part in range(2):
                        yield (1.9, 3.1, 4.3, 6.6)[2 * half + part]
                        if not half and not part:
                            on(pe, od, t, "catT")
                        if half and not part:
                            on(pe, od, t, "x2a")
                        for k in range(4 * part, 4 * part + 4):
                            last = mm(OB.ap(), catT[:, k, :], w_out[:, k, half * 512:(half + 1) * 512],
                                      start=(k == 0), stop=(k == KD - 1))
                    done(op, f"out{half}", last)
            run_tiles(front, core, attend, finish)


IN_SHAPES = dict(
    x_prompt=(SEQ, D), x_sample=(DEC, D), cache_k=(WINDOW, AT_W), cache_v=(WINDOW, AT_W),
    conv_state=(P, CONV_BLOCKS, HALO), state=(H_DN, DK, DK), ln1=(P, KD), w_in=(D, IN_W),
    conv_w=(P, CONV_BLOCKS, CONV_W), a_log=(1, H_DN), dt_bias=(1, H_DN), dn_norm=(DK, 1), q_norm=(1, DH),
    k_norm=(1, DH), rel_bias=(H_AT, N_REL), attn_norm=(P, AT_W // P), w_out=(D, D), ln2=(P, KD),
    wq=(2 * PH, P, KD, P), keys=(P, 2 * PH, NK), u=(GROUPS, P, JG, KD, P), v=(GROUPS, P, JG, D), consts=(P, C_END))
OUT_SHAPES = dict(
    y_prompt=(SEQ, D), y_sample=(DEC, D), p_k=(WINDOW, AT_W), p_v=(WINDOW, AT_W), p_conv=(HALO, CONV_CH),
    p_state=(H_DN, DK, DK), s_k=(DEC, AT_W), s_v=(DEC, AT_W), s_conv=(HALO, CONV_CH), s_state=(H_DN, DK, DK))


def rows(prompt, sample):
    return lambda t: prompt[t * P:(t + 1) * P, :] if t < PT else sample


def layer(nc, I, O):
    proj = nc.dram_tensor("proj", [PADTOK, IN_W], F32, kind="Internal").ap()
    toeplitz = nc.dram_tensor("toeplitz", [H_AT, TOE], F32, kind="Internal").ap()
    x2 = nc.dram_tensor("x2", [TOK, D], F32, kind="Internal").ap()
    gates = nc.dram_tensor("gates", [GROUPS, P, NB, JG * GB], F32, kind="Internal").ap()
    x_tile = rows(I["x_prompt"], I["x_sample"])
    x2_tile = rows(x2, x2[SEQ:TOK, :])
    ident_d, eps_d = I["consts"][:, C_IDENT:C_IDENT + P], I["consts"][:, C_EPS:C_EPS + 1]
    iota_d = I["consts"][:, C_IOTA:C_IOTA + P]
    with nc.sbuf_tensor("band_bias", [P, H_AT, BAND], F32) as bias:
        project(nc, I, x_tile, proj, toeplitz, bias)
        mix(nc, I, proj, x_tile, x2_tile, O, bias)
    with nc.sbuf_tensor("h2_hi", [P, KD, TOK], F32R) as h_hi, nc.sbuf_tensor("h2_lo", [P, KD, TOK], F32R) as h_lo:
        normed_transposed(nc, "n2", x2_tile, I["ln2"], h_hi, h_lo, ident_d, eps_d)
        with nc.sbuf_tensor("sel_i", [P, PADTOK], F32) as sel_i, nc.sbuf_tensor("sel_j", [P, PADTOK], F32) as sel_j, \
                nc.sbuf_tensor("sel_g", [P, PADTOK], F32) as sel_g:
            route(nc, h_hi, h_lo, I["wq"], I["keys"], ident_d, iota_d[:, 0:TOPK],
                  I["consts"][:, C_STARTS:C_STARTS + TOPK], sel_i, sel_j, sel_g)
            gate_matrices(nc, sel_i, sel_j, sel_g, iota_d, gates)
        experts(nc, h_hi, h_lo, gates, I["u"], I["v"], x2_tile, ident_d, rows(O["y_prompt"], O["y_sample"]))


def laid_out(inputs):
    a = {k: np.asarray(v)[0] for k, v in inputs.items()}

    def blocks(x):
        return x.reshape(-1, P).T
    return dict(
        x_prompt=a["x_prompt"], x_sample=a["x_sample"], cache_k=a["cache_attn_k"][0].reshape(WINDOW, AT_W),
        cache_v=a["cache_attn_v"][0].reshape(WINDOW, AT_W),
        conv_state=a["state_dn_conv"][0].reshape(HALO, CONV_BLOCKS, P).transpose(2, 1, 0), state=a["state_dn"][0],
        ln1=blocks(a["ln1"]), w_in=a["w_in"], conv_w=a["conv_w"].reshape(CONV_W, CONV_BLOCKS, P).transpose(2, 1, 0),
        a_log=a["a_log"][None], dt_bias=a["dt_bias"][None], dn_norm=a["dn_norm"][:, None], q_norm=a["q_norm"][None],
        k_norm=a["k_norm"][None], rel_bias=a["rel_bias"][:, ::-1], attn_norm=blocks(a["attn_norm"]),
        w_out=a["w_out"], ln2=blocks(a["ln2"]),
        wq=a["peer_wq"].reshape(KD, P, 2 * PH, P).transpose(2, 1, 0, 3),
        keys=a["peer_keys"].reshape(2 * PH, NK, P).transpose(2, 0, 1),
        u=a["peer_u"].reshape(NK, GROUPS, JG, KD, P).transpose(1, 4, 2, 3, 0),
        v=a["peer_v"].reshape(NK, GROUPS, JG, D).transpose(1, 0, 2, 3), consts=constants())


def kernel(**inputs):
    import concourse.bacc as bacc
    from concourse.bass_utils import run_bass_kernel_spmd

    arrays = {f"in_{k}": np.ascontiguousarray(v) for k, v in laid_out(inputs).items()}
    nc = bacc.Bacc("TRN2", target_bir_lowering=False, num_devices=1)
    I = {k: nc.dram_tensor(f"in_{k}", shape, F32, kind="ExternalInput").ap() for k, shape in IN_SHAPES.items()}
    O = {k: nc.dram_tensor(f"out_{k}", shape, F32, kind="ExternalOutput").ap() for k, shape in OUT_SHAPES.items()}
    layer(nc, I, O)
    r = run_bass_kernel_spmd(nc, [arrays], core_ids=[0]).results[0]
    o = {k: np.asarray(r[f"out_{k}"]) for k in OUT_SHAPES}
    return (o["y_prompt"][None], o["y_sample"][None],
            o["p_k"].reshape(1, 1, WINDOW, H_AT, DH), o["p_v"].reshape(1, 1, WINDOW, H_AT, DH),
            o["p_conv"][None, None], o["p_state"][None, None],
            o["s_k"].reshape(1, 1, DEC, H_AT, DH), o["s_v"].reshape(1, 1, DEC, H_AT, DH),
            o["s_conv"][None, None], o["s_state"][None, None])
```
